# Optimizing a Trainium2 kernel written in Bass

```python
import math
import jax, jax.numpy as jnp
from jax import lax
import numpy as np

D_MODEL = 1024
BATCH = 1
SEQ = 1024
DEPTH = 1

D_MIX = D_MODEL
GLA_HEADS = 4
GLA_DV = D_MIX // 2 // GLA_HEADS
GLA_DK = GLA_DV // 2
GLA_RANK = 16
GLA_GATE_TAU = 16.0
GLA_CHUNK = 64
SWA_HEADS = 8
SWA_KV_HEADS = 2
SWA_HEAD_DIM = D_MIX // 2 // SWA_HEADS
SWA_WINDOW = 128
N_EXPERTS = 32
TOP_K = 4
D_FF = D_MODEL
SWIGLU_LIMIT = 7.0
SWIGLU_ALPHA = 1.702
MOE_BLOCK = 128
NORM_EPS = 1e-5

SPLIT_SIZES = (
    GLA_HEADS * GLA_DK,
    GLA_HEADS * GLA_DK,
    GLA_HEADS * GLA_DV,
    GLA_HEADS * GLA_DV,
    GLA_RANK,
    SWA_HEADS * SWA_HEAD_DIM,
    SWA_KV_HEADS * SWA_HEAD_DIM,
    SWA_KV_HEADS * SWA_HEAD_DIM,
)
D_IN = sum(SPLIT_SIZES)
D_CAT = GLA_HEADS * GLA_DV + SWA_HEADS * SWA_HEAD_DIM

kernel_name = "hymba_gla_swa_sink_moe"

def rmsnorm(x, g):
    xf = x.astype(jnp.float32)
    y = xf * lax.rsqrt(jnp.mean(xf * xf, axis=-1, keepdims=True) + NORM_EPS)
    return (y * g.astype(jnp.float32)).astype(x.dtype)

def alibi_slopes(n):
    return jnp.exp2(-8.0 * jnp.arange(1, n + 1, dtype=jnp.float32) / n)

def gla_chunked(q, k, v, log_a):
    B, L, H, dk = q.shape
    dv = v.shape[-1]
    C = GLA_CHUNK
    n = L // C

    def to_chunks(t):
        return jnp.moveaxis(t.astype(jnp.float32).reshape(B, n, C, H, t.shape[-1]), 1, 0)

    qc, kc, vc, gc = (to_chunks(t) for t in (q * (dk ** -0.5), k, v, log_a))
    causal = jnp.tril(jnp.ones((C, C), dtype=bool))

    def step(S, inp):
        qi, ki, vi, gi = inp
        b = jnp.cumsum(gi, axis=1)
        b_last = b[:, -1]
        q_e = qi * jnp.exp(b)
        k_e = ki * jnp.exp(-b)
        A = jnp.where(causal, jnp.einsum('bihd,bjhd->bhij', q_e, k_e), 0.0)
        o = (jnp.einsum('bhij,bjhv->bihv', A, vi)
             + jnp.einsum('bihd,bhdv->bihv', q_e, S))
        k_tail = ki * jnp.exp(b_last[:, None] - b)
        S = jnp.exp(b_last)[..., None] * S + jnp.einsum('bjhd,bjhv->bhdv', k_tail, vi)
        return S, o

    S0 = jnp.zeros((B, H, dk, dv), jnp.float32)
    _, o = lax.scan(step, S0, (qc, kc, vc, gc))
    return jnp.moveaxis(o, 0, 1).reshape(B, L, H, dv).astype(v.dtype)

def swa_with_sinks(q, k, v, sinks, slopes):
    B, L, Hq, dh = q.shape
    Hkv = k.shape[2]
    G = Hq // Hkv
    W = SWA_WINDOW
    nb = L // W
    qb = q.reshape(B, nb, W, Hkv, G, dh)

    def band(t):
        tb = t.reshape(B, nb, W, Hkv, dh)
        prev = jnp.concatenate([jnp.zeros_like(tb[:, :1]), tb[:, :-1]], axis=1)
        return jnp.concatenate([prev, tb], axis=2)

    kb, vb = band(k), band(v)
    s = jnp.einsum('bnqkgd,bnskd->bnkgqs', qb, kb).astype(jnp.float32) * (dh ** -0.5)
    rel = jnp.arange(W)[:, None] + W - jnp.arange(2 * W)[None, :]
    in_window = (rel >= 0) & (rel < W)
    exists = (jnp.arange(nb)[:, None] > 0) | (jnp.arange(2 * W)[None, :] >= W)
    valid = in_window[None] & exists[:, None, :]
    bias = -slopes.reshape(Hkv, G)[:, :, None, None] * rel.astype(jnp.float32)
    s = jnp.where(valid[None, :, None, None], s + bias, -jnp.inf)
    sink = jnp.broadcast_to(sinks.astype(jnp.float32).reshape(1, 1, Hkv, G, 1, 1),
                            s.shape[:-1] + (1,))
    p = jax.nn.softmax(jnp.concatenate([s, sink], axis=-1), axis=-1)[..., :-1]
    o = jnp.einsum('bnkgqs,bnskd->bnqkgd', p.astype(v.dtype), vb)
    return o.reshape(B, L, Hq * dh)

def moe(h, w_router, b_router, w_glu, b_glu, w_lin, b_lin, w_down, b_down):
    T, D = h.shape
    TK = T * TOP_K
    logits = (h @ w_router + b_router).astype(jnp.float32)
    top_val, top_idx = lax.top_k(logits, TOP_K)
    gate = jax.nn.softmax(top_val, axis=-1)

    flat_e = top_idx.reshape(-1)
    flat_tok = jnp.repeat(jnp.arange(T, dtype=jnp.int32), TOP_K)
    flat_w = gate.reshape(-1)
    order = jnp.argsort(flat_e)
    e_sorted = flat_e[order]
    counts = jnp.bincount(flat_e, length=N_EXPERTS)
    starts = jnp.cumsum(counts) - counts
    padded = (counts + MOE_BLOCK - 1) // MOE_BLOCK * MOE_BLOCK
    pends = jnp.cumsum(padded)
    pstarts = pends - padded
    dest = pstarts[e_sorted] + (jnp.arange(TK) - starts[e_sorted])

    n_blocks = -(-TK // MOE_BLOCK) + N_EXPERTS
    P = n_blocks * MOE_BLOCK
    tok_buf = jnp.zeros((P,), jnp.int32).at[dest].set(flat_tok[order])
    w_buf = jnp.zeros((P,), jnp.float32).at[dest].set(flat_w[order])
    block_expert = jnp.minimum(
        jnp.searchsorted(pends, jnp.arange(n_blocks) * MOE_BLOCK, side='right'), N_EXPERTS - 1)
    xb = h[tok_buf].reshape(n_blocks, MOE_BLOCK, D)

    def expert_block(args):
        xblk, e = args
        glu = jnp.minimum(xblk @ w_glu[e] + b_glu[e], SWIGLU_LIMIT)
        lin = jnp.clip(xblk @ w_lin[e] + b_lin[e], -SWIGLU_LIMIT, SWIGLU_LIMIT)
        hid = glu * jax.nn.sigmoid(SWIGLU_ALPHA * glu) * (lin + 1.0)
        return hid @ w_down[e] + b_down[e]

    y = lax.map(expert_block, (xb, block_expert)).reshape(P, D)
    return jnp.zeros_like(h).at[tok_buf].add(y * w_buf[:, None].astype(h.dtype))

def setup_inputs(seed: int = 0) -> dict:
    key = jax.random.key(seed)
    ks = jax.random.split(key, 20)
    f32 = jnp.float32

    def nrm(k, shape, scale):
        return jax.random.normal(k, shape, f32) * scale

    Ly = DEPTH
    return {
        "x": nrm(ks[0], (BATCH, SEQ, D_MODEL), 1.0),
        "norm1_g": 1.0 + nrm(ks[1], (Ly, D_MODEL), 0.02),
        "w_in": nrm(ks[2], (Ly, D_MODEL, D_IN), D_MODEL ** -0.5),
        "w_alpha_up": nrm(ks[3], (Ly, GLA_RANK, GLA_HEADS * GLA_DK), GLA_RANK ** -0.5),
        "b_alpha": nrm(ks[4], (Ly, GLA_HEADS * GLA_DK), 0.1) + 2.0,
        "gla_norm_g": 1.0 + nrm(ks[5], (Ly, GLA_DV), 0.02),
        "swa_sinks": nrm(ks[6], (Ly, SWA_HEADS), 0.5),
        "swa_norm_g": 1.0 + nrm(ks[7], (Ly, SWA_HEAD_DIM), 0.02),
        "w_out": nrm(ks[8], (Ly, D_CAT, D_MODEL), D_CAT ** -0.5),
        "norm2_g": 1.0 + nrm(ks[9], (Ly, D_MODEL), 0.02),
        "w_router": nrm(ks[10], (Ly, D_MODEL, N_EXPERTS), D_MODEL ** -0.5),
        "b_router": nrm(ks[11], (Ly, N_EXPERTS), 0.01),
        "w_glu": nrm(ks[12], (Ly, N_EXPERTS, D_MODEL, D_FF), D_MODEL ** -0.5),
        "b_glu": nrm(ks[13], (Ly, N_EXPERTS, D_FF), 0.01),
        "w_lin": nrm(ks[14], (Ly, N_EXPERTS, D_MODEL, D_FF), D_MODEL ** -0.5),
        "b_lin": nrm(ks[15], (Ly, N_EXPERTS, D_FF), 0.01),
        "w_down": nrm(ks[16], (Ly, N_EXPERTS, D_FF, D_MODEL), D_FF ** -0.5),
        "b_down": nrm(ks[17], (Ly, N_EXPERTS, D_MODEL), 0.01),
        "final_g": 1.0 + nrm(ks[18], (D_MODEL,), 0.02),
    }

def reference(x, norm1_g, w_in, w_alpha_up, b_alpha, gla_norm_g, swa_sinks, swa_norm_g,
              w_out, norm2_g, w_router, b_router, w_glu, b_glu, w_lin, b_lin,
              w_down, b_down, final_g):
    B, L, D = x.shape
    offsets = [int(o) for o in np.cumsum(SPLIT_SIZES)[:-1]]
    slopes = alibi_slopes(SWA_HEADS)
    h = x
    for l in range(DEPTH):
        u = rmsnorm(h, norm1_g[l])
        proj = u @ w_in[l]
        q_a, k_a, v_a, r_a, z_a, q_b, k_b, v_b = jnp.split(proj, offsets, axis=-1)
        log_a = jax.nn.log_sigmoid(
            (z_a @ w_alpha_up[l] + b_alpha[l]).astype(jnp.float32)) / GLA_GATE_TAU
        o_a = gla_chunked(q_a.reshape(B, L, GLA_HEADS, GLA_DK),
                          k_a.reshape(B, L, GLA_HEADS, GLA_DK),
                          v_a.reshape(B, L, GLA_HEADS, GLA_DV),
                          log_a.reshape(B, L, GLA_HEADS, GLA_DK))
        o_a = rmsnorm(o_a, gla_norm_g[l]).reshape(B, L, GLA_HEADS * GLA_DV) * jax.nn.silu(r_a)
        o_b = swa_with_sinks(q_b.reshape(B, L, SWA_HEADS, SWA_HEAD_DIM),
                             k_b.reshape(B, L, SWA_KV_HEADS, SWA_HEAD_DIM),
                             v_b.reshape(B, L, SWA_KV_HEADS, SWA_HEAD_DIM),
                             swa_sinks[l], slopes)
        o_b = rmsnorm(o_b.reshape(B, L, SWA_HEADS, SWA_HEAD_DIM),
                      swa_norm_g[l]).reshape(B, L, SWA_HEADS * SWA_HEAD_DIM)
        h = h + jnp.concatenate([o_a, o_b], axis=-1) @ w_out[l]
        hn = rmsnorm(h, norm2_g[l]).reshape(B * L, D)
        h = h + moe(hn, w_router[l], b_router[l], w_glu[l], b_glu[l], w_lin[l], b_lin[l],
                    w_down[l], b_down[l]).reshape(B, L, D)
    return rmsnorm(h, final_g)


_drawn_inputs = setup_inputs


def setup_inputs(seed=0):
    import zlib

    import numpy as np

    out = dict(_drawn_inputs(seed))
    spreads = {}
    factors = {'swa_sinks': 8.0, 'b_glu': 8.0, 'b_lin': 22.288, 'b_down': 8.0, 'final_g': 8.439}
    for name, (base, spread) in spreads.items():
        noise = np.random.default_rng([zlib.crc32(name.encode()), seed]).standard_normal(out[name].shape)
        drawn = base * np.exp(spread * noise) if base else spread * noise
        out[name] = __import__('jax').numpy.asarray(drawn.astype(out[name].dtype))
    for name, factor in factors.items():
        out[name] = (out[name] * factor).astype(out[name].dtype)
    return out
```

```python
from contextlib import ExitStack

import concourse.bass as bass
from concourse import mybir

F32, F32R = mybir.dt.float32, mybir.dt.float32r
I32, U32 = mybir.dt.int32, mybir.dt.uint32
ALU, ACT = mybir.AluOpType, mybir.ActivationFunctionType
AX_X = mybir.AxisListType.X

P = 128
SEQ, D = 1024, 1024
TILES = SEQ // P
KT = D // P
EPS = 1e-5

GLA_HEADS, GLA_DK, GLA_DV, RANK, CHUNK, TAU = 4, 64, 128, 16, 64, 16.0
PAIRS = GLA_HEADS // 2
CHUNKS = SEQ // CHUNK
SWA_HEADS, KV_HEADS, DH, WINDOW = 8, 2, 64, 128
GROUP = SWA_HEADS // KV_HEADS

QA, KA = 0, GLA_HEADS * GLA_DK
VA = 2 * KA
RA = VA + GLA_HEADS * GLA_DV
ZA = RA + GLA_HEADS * GLA_DV
QB = ZA + RANK
KB = QB + SWA_HEADS * DH
VB = KB + KV_HEADS * DH
VZ = KV_HEADS * DH + RANK

EXPERTS, TOP_K, DFF, LIMIT, ALPHA = 32, 4, 1024, 7.0, 1.702
GROUP_ROWS = 2 * P
MAX_GROUPS = (TOP_K * SEQ + EXPERTS * (GROUP_ROWS - 1)) // GROUP_ROWS
GROUPS = MAX_GROUPS + 1
BLOCKS = 2 * GROUPS
SPARE = TOP_K * SEQ


def project(nc, x, norm1_g, w_in, ident, qaT, kaT, va, ra, qbT, kbT, vbz):
    HALF = KT // 2
    SLOTS = 4
    units = [
        ([(QA, 256)], True), ([(KA, 256)], True), ([(VB, 128), (ZA, RANK)], False),
        ([(VA, 256)], False), ([(VA + 256, 256)], False),
        ([(QB + DH * h, DH) for h in (0, 4, 1, 5)], True), ([(QB + DH * h, DH) for h in (2, 6, 3, 7)], True),
        ([(KB, 128)], True),
        ([(RA, 256)], False), ([(RA + 256, 256)], False),
    ]
    with ExitStack() as ctx:
        def sb(name, shape, dt=F32):
            return ctx.enter_context(nc.sbuf_tensor(name, shape, dt))

        def sem(name):
            return ctx.enter_context(nc.semaphore(name))

        uTh, uTl = sb("uTh", [P, KT, SEQ], F32R), sb("uTl", [P, KT, SEQ], F32R)
        raw = sb("w_in_raw", [P, SLOTS, HALF, 256])
        wh, wl = sb("w_in_hi", [P, SLOTS, HALF, 256], F32R), sb("w_in_lo", [P, SLOTS, HALF, 256], F32R)
        xt, xn = sb("x_tile", [P, 2, D]), sb("x_normed", [P, 2, D])
        g1 = sb("norm1_rows", [P, D])
        ss, rms, rstd = sb("x_ss", [P, TILES]), sb("x_rms", [P, TILES]), sb("x_rstd", [P, TILES])
        eps = sb("eps1", [P, 1])
        pT = [ctx.enter_context(nc.psum_tensor(f"uT_ps{i}", [P, 512], F32)) for i in range(2)]
        OB = 6
        pO = [ctx.enter_context(nc.psum_tensor(f"proj_ps{i}", [P, 512], F32)) for i in range(OB)]

        x_loaded = [sem(f"x_loaded{i}") for i in range(2)]
        g1_loaded, eps_set, w_loaded = sem("g1_loaded"), sem("eps1_set"), [sem(f"w_in_loaded{i}") for i in range(SLOTS)]
        summed, rooted, inverted, normed = sem("x_summed"), sem("x_rooted"), sem("x_inverted"), sem("x_normed_s")
        uT_turned, uT_hi, uT_lo = sem("uT_turned"), sem("uT_hi"), sem("uT_lo")
        w_hi, w_lo, unit_done = sem("w_in_hi_s"), sem("w_in_lo_s"), sem("unit_done")
        out_done, act_out, dve_out = sem("proj_out_done"), sem("proj_act_out"), sem("proj_dve_out")

        w_rows = w_in.rearrange("(k p) n -> p k n", p=P)
        x_rows = x.rearrange("(t p) d -> t p d", p=P)

        outs = []
        for u, (cols, turned) in enumerate(units):
            if turned:
                for c in range(1 if u == 7 else 2):
                    for half in range(2):
                        dst = {0: qaT, 1: kaT, 5: qbT, 6: qbT, 7: kbT}[u]
                        row = c + (2 if u == 6 else 0)
                        outs.append((u, c, half, dst[:, row, half * 512:half * 512 + 512], 512))
            else:
                for t in range(TILES):
                    dst = {2: vbz[:, t, :], 3: va[:, t, 0:256], 4: va[:, t, 256:512], 8: ra[:, t, 0:256], 9: ra[:, t, 256:512]}[u]
                    outs.append((u, None, t, dst, VZ if u == 2 else 256))
        first_out = [min(n for n, o in enumerate(outs) if o[0] == u) for u in range(len(units))] + [len(outs)]

        with nc.Block() as block:
            @block.sync
            def _(sp):
                for t in range(TILES):
                    if t >= 2:
                        sp.wait_ge(normed, t - 1)
                        sp.wait_ge(summed, t - 1)
                    sp.dma_start(xt[:, t % 2, :], x_rows[t]).then_inc(x_loaded[t % 2], 16)
                    if t == 0:
                        sp.dma_start(g1[:], norm1_g.partition_broadcast(P)).then_inc(g1_loaded, 16)

            @block.gpsimd
            def _(pool):
                for u, (cols, _) in enumerate(units):
                    for half in range(2):
                        h = 2 * u + half
                        if h >= SLOTS:
                            pool.wait_ge(w_lo, h - SLOTS + 1)
                        at = 0
                        for c0, n in cols:
                            pool.dma_start(raw[:, h % SLOTS, :, at:at + n],
                                           w_rows[:, half * HALF:(half + 1) * HALF, c0:c0 + n]).then_inc(w_loaded[h % SLOTS], 16)
                            at += n

            def arrived(h):
                return 16 * sum(len(units[g // 2][0]) for g in range(h % SLOTS, h + 1, SLOTS))

            def width(u):
                return sum(n for _, n in units[u][0])

            @block.scalar
            def _(act):
                act.wait_ge(eps_set, 1)
                for t in range(TILES):
                    act.wait_ge(x_loaded[t % 2], 16 * (t // 2 + 1))
                    if t >= 2:
                        act.wait_ge(uT_turned, 2 * (t - 1))
                    nc.scalar.activation(xn[:, t % 2, :], xt[:, t % 2, :], ACT.Square, accum_out=ss[:, t:t + 1]).then_inc(summed, 1)
                    act.wait_ge(summed, t + 1)
                    nc.scalar.activation(rms[:, t:t + 1], ss[:, t:t + 1], ACT.Sqrt, bias=eps[:], scale=1.0 / D).then_inc(rooted, 1)
                    for half in range(2):
                        act.wait_ge(uT_turned, 2 * t + half + 1)
                        nc.scalar.activation(uTh[:, half * 4:half * 4 + 4, t * P:(t + 1) * P],
                                             pT[half][:].rearrange("p (k n) -> p k n", k=4), ACT.Copy).then_inc(uT_hi, 1)

                def split(h):
                    act.wait_ge(w_loaded[h % SLOTS], arrived(h))
                    if h >= SLOTS:
                        act.wait_ge(unit_done, (h - SLOTS) // 2 + 1)
                    n = width(h // 2)
                    nc.scalar.activation(wh[:, h % SLOTS, :, 0:n], raw[:, h % SLOTS, :, 0:n], ACT.Copy).then_inc(w_hi, 1)

                for h in range(SLOTS):
                    split(h)
                for u in range(len(units)):
                    for n in range(first_out[u], first_out[u + 1]):
                        if n % 2 == 0:
                            act.wait_ge(out_done, n + 1)
                            nc.scalar.activation(outs[n][3], pO[n % OB][:, 0:outs[n][4]], ACT.Copy).then_inc(act_out, 1)
                    for h in (2 * u + SLOTS, 2 * u + SLOTS + 1):
                        if h < 2 * len(units):
                            split(h)

            @block.vector
            def _(dve):
                nc.vector.memset(eps[:], EPS).then_inc(eps_set, 1)
                dve.wait_ge(g1_loaded, 16)
                for t in range(TILES):
                    dve.wait_ge(rooted, t + 1)
                    nc.vector.reciprocal(rstd[:, t:t + 1], rms[:, t:t + 1]).then_inc(inverted, 1)
                    dve.wait_ge(inverted, t + 1)
                    if t >= 2:
                        dve.wait_ge(uT_turned, 2 * (t - 1))
                    nc.vector.scalar_tensor_tensor(out=xn[:, t % 2, :], in0=xt[:, t % 2, :], scalar=rstd[:, t:t + 1], in1=g1[:],
                                                   op0=ALU.mult, op1=ALU.mult).then_inc(normed, 1)
                    for half in range(2):
                        dve.wait_ge(uT_hi, 2 * t + half + 1)
                        nc.vector.tensor_tensor(uTl[:, half * 4:half * 4 + 4, t * P:(t + 1) * P],
                                                pT[half][:].rearrange("p (k n) -> p k n", k=4),
                                                uTh[:, half * 4:half * 4 + 4, t * P:(t + 1) * P].bitcast(F32),
                                                ALU.subtract).then_inc(uT_lo, 1)

                def split(h):
                    dve.wait_ge(w_hi, h + 1)
                    n = width(h // 2)
                    nc.vector.tensor_tensor(wl[:, h % SLOTS, :, 0:n], raw[:, h % SLOTS, :, 0:n],
                                            wh[:, h % SLOTS, :, 0:n].bitcast(F32), ALU.subtract).then_inc(w_lo, 1)

                for h in range(SLOTS):
                    split(h)
                for u in range(len(units)):
                    for n in range(first_out[u], first_out[u + 1]):
                        if n % 2:
                            dve.wait_ge(out_done, n + 1)
                            nc.vector.tensor_copy(outs[n][3], pO[n % OB][:, 0:outs[n][4]]).then_inc(dve_out, 1)
                    for h in (2 * u + SLOTS, 2 * u + SLOTS + 1):
                        if h < 2 * len(units):
                            split(h)

            @block.tensor
            def _(pe):
                for t in range(TILES):
                    pe.wait_ge(normed, t + 1)
                    for half in range(2):
                        if t:
                            pe.wait_ge(uT_lo, 2 * (t - 1) + half + 1)
                        for k in range(4):
                            c = (half * 4 + k) * P
                            last = nc.tensor.transpose(pT[half][:, k * P:(k + 1) * P], xn[:, t % 2, c:c + P], ident[:])
                        last.then_inc(uT_turned, 1)
                pe.wait_ge(uT_lo, 2 * TILES)
                for n, (u, c, at, _, wide) in enumerate(outs):
                    if n == first_out[u]:
                        pe.wait_ge(w_lo, 2 * u + 2)
                    if n >= OB:
                        m = n - OB
                        pe.wait_ge(act_out if m % 2 == 0 else dve_out, m // 2 + 1)
                    acc = pO[n % OB][:, 0:wide]
                    for k in range(KT):
                        slot, kk = (2 * u + k // HALF) % SLOTS, k % HALF
                        if c is None:
                            rh, rl = (w[:, slot, kk, 0:wide] for w in (wh, wl))
                            sh, sl = (w[:, k, at * P:(at + 1) * P] for w in (uTh, uTl))
                        else:
                            rh, rl = (w[:, k, at * 512:at * 512 + 512] for w in (uTh, uTl))
                            sh, sl = (w[:, slot, kk, c * P:(c + 1) * P] for w in (wh, wl))
                        nc.tensor.matmul(acc, sh, rh, start=(k == 0), stop=False)
                        nc.tensor.matmul(acc, sh, rl, start=False, stop=False)
                        mm = nc.tensor.matmul(acc, sl, rh, start=False, stop=(k == KT - 1))
                    mm.then_inc(out_done, 1)
                    if n == first_out[u + 1] - 1:
                        pe.wait_ge(out_done, n + 1)
                        pe.sem_inc(unit_done, 1)


def gla(nc, w_alpha_up, b_alpha, ident, qaT, kaT, va, vbz, cat):
    with ExitStack() as ctx:
        def sb(name, shape, dt=F32):
            return ctx.enter_context(nc.sbuf_tensor(name, shape, dt))

        def sem(name):
            return ctx.enter_context(nc.semaphore(name))

        zT = sb("zT", [RANK, SEQ])
        w_up, b_up = sb("w_alpha", [RANK, PAIRS * P]), sb("b_alpha", [P, PAIRS])
        soft, gate, cum = (sb(n, [P, PAIRS, SEQ]) for n in ("softplus", "log_gate", "log_gate_sum"))
        grow, shrink = sb("exp_sum", [P, PAIRS, SEQ]), sb("exp_minus_sum", [P, PAIRS, SEQ])
        tail = soft
        kt = sb("k_tail", [P, TILES, PAIRS * P])
        restart = sb("chunk_restart", [P, SEQ])
        decay = sb("chunk_decay", [P, PAIRS, CHUNKS])
        states = [gate[:].rearrange("p a (c v) -> p (a c) v", v=GLA_DV), cum[:].rearrange("p a (c v) -> p (a c) v", v=GLA_DV)]
        causal = sb("causal", [P, GLA_HEADS, P], I32)
        ones = sb("ones_i", [P, GLA_HEADS, P], I32)
        att = sb("gla_scores", [P, 2, GLA_HEADS * P])
        ps = ctx.enter_context(nc.psum_tensor("gla_ps", [P, 8, 512], F32))

        def kv_bank(t, c):
            return (2 if t % 2 == 0 else 0) + c

        loaded, restart_set, causal_set, att_zeroed = sem("alpha_loaded"), sem("restart_set"), sem("causal_set"), sem("att_zeroed")
        z_turned, z_copied, pre_ready = sem("z_turned"), sem("z_copied"), sem("pre_ready")
        absed, softed, clipped, gated, summed, shifted = (sem(n) for n in ("abs_s", "soft_s", "clip_s", "gate_s", "sum_s", "shift_s"))
        grown, shrunk, tailed = sem("grow_s"), sem("shrink_s"), sem("tail_s")
        q_ready, kt_ready, k_ready, decay_ready = sem("q_ready"), sem("kt_ready"), sem("k_ready"), sem("decay_ready")
        kt_turned, kt_copied, kv_ready, state_ready = sem("kt_turned"), sem("kt_copied"), sem("kv_ready"), sem("state_ready")
        att_ready, att_masked, o_ready, o_copied = sem("att_ready"), sem("att_masked"), sem("o_ready"), sem("o_copied")

        with nc.Block() as block:
            @block.sync
            def _(sp):
                sp.dma_start(w_up[:], w_alpha_up).then_inc(loaded, 16)
                with nc.allow_non_contiguous_dma(reason="256 biases, one to a partition"):
                    sp.dma_start(b_up[:], b_alpha.rearrange("(c p) -> p c", p=P)).then_inc(loaded, 16)

            @block.gpsimd
            def _(pool):
                nc.gpsimd.memset(restart[:], 1.0).then_inc(restart_set, 1)
                pool.wait_ge(restart_set, 1)
                nc.gpsimd.memset(restart[:].rearrange("p (c n) -> p c n", n=CHUNK)[:, :, 0:1], 0.0).then_inc(restart_set, 1)
                nc.gpsimd.memset(ones[:], 1).then_inc(causal_set, 1)
                pool.wait_ge(causal_set, 1)
                nc.gpsimd.affine_select(out=causal[:], in_=ones[:], compare_op=ALU.is_ge, fill=0, base=0,
                                        pattern=[[0, GLA_HEADS], [1, P]], channel_multiplier=-1).then_inc(causal_set, 1)
                pool.wait_ge(causal_set, 2)
                nc.gpsimd.memset(causal[0:CHUNK, :, CHUNK:P], 0).then_inc(causal_set, 1)
                nc.gpsimd.memset(att[:], 0.0).then_inc(att_zeroed, 1)

            @block.scalar
            def _(act):
                act.wait_ge(loaded, 32)
                for c in range(PAIRS):
                    act.wait_ge(pre_ready, 2 * c + 2)
                    nc.scalar.activation(soft[:, c, :], ps[:, 2 + 2 * c:4 + 2 * c, :], ACT.Abs, bias=b_up[:, c:c + 1]).then_inc(absed, 1)
                for c in range(PAIRS):
                    act.wait_ge(absed, c + 1)
                    nc.scalar.activation(soft[:, c, :], soft[:, c, :], ACT.Exp, scale=-1.0).then_inc(softed, 1)
                    act.wait_ge(softed, 2 * c + 1)
                    nc.scalar.activation(soft[:, c, :], soft[:, c, :], ACT.Ln, bias=1.0).then_inc(softed, 1)
                for c in range(PAIRS):
                    act.wait_ge(summed, c + 1)
                    nc.scalar.activation(grow[:, c, :], cum[:, c, :], ACT.Exp, scale=1.0 / TAU).then_inc(grown, 1)
                    act.wait_ge(shifted, c + 1)
                    nc.scalar.activation(tail[:, c, :], tail[:, c, :], ACT.Exp, scale=1.0 / TAU).then_inc(tailed, 1)
                    nc.scalar.activation(shrink[:, c, :], cum[:, c, :], ACT.Exp, scale=-1.0 / TAU).then_inc(shrunk, 1)
                for n in range(4):
                    act.wait_ge(kt_turned, n + 1)
                    nc.scalar.activation(kt[:, 2 * n:2 * n + 2, :], ps[:, n % 2, :].rearrange("p (t c) -> p t c", t=2), ACT.Copy).then_inc(kt_copied, 1)
                for t in range(TILES):
                    act.wait_ge(o_ready, t + 1)
                    nc.scalar.activation(cat[:, t, 0:512].rearrange("p (a b v) -> p b a v", a=PAIRS, b=2),
                                         ps[:, 6:8, 0:256].rearrange("p b (a v) -> p b a v", a=PAIRS), ACT.Copy).then_inc(o_copied, 1)

            @block.vector
            def _(dve):
                dve.wait_ge(z_turned, 1)
                nc.vector.tensor_copy(zT[:], ps[0:RANK, 0:2, :].rearrange("p b n -> p (b n)")).then_inc(z_copied, 1)
                dve.wait_ge(loaded, 32)
                for c in range(PAIRS):
                    dve.wait_ge(absed, c + 1)
                    nc.vector.tensor_scalar(gate[:, c, :], ps[:, 2 + 2 * c:4 + 2 * c, :].rearrange("p b n -> p (b n)"), b_up[:, c:c + 1], 0.0,
                                            ALU.add, ALU.min).then_inc(clipped, 1)
                for c in range(PAIRS):
                    dve.wait_ge(softed, 2 * c + 2)
                    dve.wait_ge(clipped, c + 1)
                    nc.vector.tensor_tensor(gate[:, c, :], gate[:, c, :], soft[:, c, :], ALU.subtract).then_inc(gated, 1)
                    dve.wait_ge(gated, c + 1)
                    dve.wait_ge(restart_set, 2)
                    nc.vector.tensor_tensor_scan(cum[:, c, :], restart[:], gate[:, c, :], 0.0, ALU.mult, ALU.add).then_inc(summed, 1)
                    dve.wait_ge(summed, c + 1)
                    by_chunk = cum[:, c, :].rearrange("p (c n) -> p c n", n=CHUNK)
                    nc.vector.tensor_tensor(tail[:, c, :].rearrange("p (c n) -> p c n", n=CHUNK),
                                            by_chunk[:, :, CHUNK - 1:CHUNK].to_broadcast([P, CHUNKS, CHUNK]), by_chunk,
                                            ALU.subtract).then_inc(shifted, 1)
                for c in range(PAIRS):
                    dve.wait_ge(tailed, c + 1)
                    nc.vector.tensor_tensor(tail[:, c, :], kaT[:, c, :], tail[:, c, :], ALU.mult).then_inc(kt_ready, 1)
                    dve.wait_ge(kt_ready, c + 1)
                    dve.wait_ge(shrunk, c + 1)
                    nc.vector.tensor_tensor(kaT[:, c, :], kaT[:, c, :], shrink[:, c, :], ALU.mult).then_inc(k_ready, 1)
                    dve.wait_ge(grown, c + 1)
                    nc.vector.scalar_tensor_tensor(out=qaT[:, c, :], in0=qaT[:, c, :], scalar=GLA_DK ** -0.5, in1=grow[:, c, :],
                                                   op0=ALU.mult, op1=ALU.mult).then_inc(q_ready, 1)
                    nc.vector.tensor_copy(decay[:, c, :], grow[:, c, :].rearrange("p (c n) -> p c n", n=CHUNK)[:, :, CHUNK - 1]).then_inc(decay_ready, 1)
                dve.wait_ge(decay_ready, PAIRS)
                dve.wait_ge(att_zeroed, 1)
                dve.wait_ge(causal_set, 3)

                def mask(t):
                    dve.wait_ge(att_ready, t + 1)
                    if t >= 2:
                        dve.wait_ge(o_ready, t - 1)
                    nc.vector.copy_predicated(att[:, t % 2, :].rearrange("p (b n) -> p b n", b=2), causal[:].rearrange("p (b a) n -> p b (a n)", b=2),
                                              ps[:, 4:6, 0:256]).then_inc(att_masked, 1)

                for c in range(CHUNKS):
                    if c < CHUNKS - 1:
                        if c % 2 == 0:
                            dve.wait_ge(kv_ready, c // 2 + 1)
                        for pair in range(PAIRS):
                            kv = ps[:, kv_bank(c // 2, c % 2), pair * P:(pair + 1) * P]
                            if c == 0:
                                ins = nc.vector.tensor_copy(states[pair][:, c, :], kv)
                            else:
                                dve.wait_ge(state_ready, (c - 1) * PAIRS + pair + 1)
                                ins = nc.vector.scalar_tensor_tensor(out=states[pair][:, c, :], in0=states[pair][:, c - 1, :],
                                                                     scalar=decay[:, pair, c:c + 1], in1=kv, op0=ALU.mult, op1=ALU.add)
                            ins.then_inc(state_ready, 1)
                    if c % 2 == 0:
                        mask(c // 2)

            @block.tensor
            def _(pe):
                for t in range(TILES):
                    last = nc.tensor.transpose(ps[0:RANK, t // 4, (t % 4) * P:(t % 4 + 1) * P], vbz[:, t, P:VZ], ident[:])
                last.then_inc(z_turned, 1)
                pe.wait_ge(loaded, 32)
                pe.wait_ge(z_copied, 1)
                for c in range(PAIRS):
                    for half in range(2):
                        nc.tensor.matmul(ps[:, 2 + 2 * c + half, :], w_up[:, c * P:(c + 1) * P], zT[:, half * 512:half * 512 + 512],
                                         start=True, stop=True).then_inc(pre_ready, 1)
                pe.wait_ge(kt_ready, PAIRS)
                for n in range(4):
                    if n >= 2:
                        pe.wait_ge(kt_copied, n - 1)
                    for t in (0, 1):
                        for c in range(PAIRS):
                            last = nc.tensor.transpose(ps[:, n % 2, (t * PAIRS + c) * P:(t * PAIRS + c + 1) * P],
                                                       tail[:, c, (2 * n + t) * P:(2 * n + t + 1) * P], ident[:])
                    last.then_inc(kt_turned, 1)

                def kv(t):
                    if t >= 2:
                        pe.wait_ge(state_ready, 2 * PAIRS * (t - 1))
                    pe.wait_ge(kt_copied, 4)
                    for c in (0, 1):
                        for pair in range(PAIRS):
                            for h in (0, 1):
                                head = 2 * pair + h
                                last = nc.tensor.matmul(ps[h * 64:h * 64 + 64, kv_bank(t, c), pair * P:(pair + 1) * P],
                                                        kt[c * 64:c * 64 + 64, t, pair * P + h * 64:pair * P + h * 64 + 64],
                                                        va[c * 64:c * 64 + 64, t, head * P:(head + 1) * P], start=True, stop=True)
                    last.then_inc(kv_ready, 1)

                def scores(t):
                    if t:
                        pe.wait_ge(att_masked, t)
                    pe.wait_ge(q_ready, PAIRS)
                    pe.wait_ge(k_ready, PAIRS)
                    for head in range(GLA_HEADS):
                        part = slice(head % 2 * 64, head % 2 * 64 + 64)
                        last = nc.tensor.matmul(ps[:, 4 + head % 2, head // 2 * P:(head // 2 + 1) * P], kaT[part, head // 2, t * P:(t + 1) * P],
                                                qaT[part, head // 2, t * P:(t + 1) * P], start=True, stop=True)
                    last.then_inc(att_ready, 1)

                def mix(t):
                    pe.wait_ge(att_masked, t + 1)
                    if t:
                        pe.wait_ge(o_copied, t)
                    pe.wait_ge(state_ready, min(2 * t + 1, CHUNKS - 1) * PAIRS)
                    for head in range(GLA_HEADS):
                        part = slice(head % 2 * 64, head % 2 * 64 + 64)
                        out = ps[:, 6 + head % 2, head // 2 * P:(head // 2 + 1) * P]
                        at = (head % 2 * PAIRS + head // 2) * P
                        nc.tensor.matmul(out, att[:, t % 2, at:at + P], va[:, t, head * P:(head + 1) * P], start=True, stop=False,
                                         skip_group_check=True)
                        for c in (0, 1):
                            if 2 * t + c:
                                last = nc.tensor.matmul(out[c * 64:c * 64 + 64], qaT[part, head // 2, t * P + c * 64:t * P + c * 64 + 64],
                                                        states[head // 2][part, 2 * t + c - 1, :], start=False, stop=True,
                                                        skip_group_check=True)
                    last.then_inc(o_ready, 1)

                kv(0)
                scores(0)
                for t in range(TILES):
                    if t + 1 < TILES:
                        kv(t + 1)
                        scores(t + 1)
                    mix(t)


def swa(nc, swa_sinks, ident, qbT, kbT, vbz, cat):
    units = [(n, g) for n in range(TILES) for g in range(KV_HEADS)]
    with ExitStack() as ctx:
        def sb(name, shape, dt=F32):
            return ctx.enter_context(nc.sbuf_tensor(name, shape, dt))

        def sem(name):
            return ctx.enter_context(nc.semaphore(name))

        rel = sb("distance", [P, 2 * WINDOW])
        bias = sb("alibi", [P, SWA_HEADS, 2 * WINDOW])
        sink = sb("sinks", [P, SWA_HEADS])
        s = sb("swa_scores", [P, 2, GROUP, 2 * WINDOW])
        pT = sb("swa_probs_T", [P, 2, GROUP * P])
        top, low, es = sb("swa_max", [P, 2, GROUP]), sb("swa_minus_max", [P, 2, GROUP]), sb("sink_exp", [P, 2, GROUP])
        den = sb("swa_sum", [P, 2, GROUP])
        ps_s = [ctx.enter_context(nc.psum_tensor(f"swa_s{i}", [P, GROUP, 2 * WINDOW], F32)) for i in range(2)]
        ps_t = [ctx.enter_context(nc.psum_tensor(f"swa_t{i}", [P, GROUP * P], F32)) for i in range(2)]
        ps_o = [ctx.enter_context(nc.psum_tensor(f"swa_o{i}", [P, 512], F32)) for i in range(2)]

        sinks_loaded, rel_done, sloped, bias_done = sem("sinks_loaded"), sem("rel_done"), sem("sloped"), sem("alibi_done")
        scored, biased, maxed, topped, lowed = (sem(n) for n in ("scored", "biased", "maxed", "topped", "lowed"))
        exped, sink_shifted, sink_exped, summed, inverted = (sem(n) for n in ("exped", "sink_shifted", "sink_exped", "swa_summed", "swa_inverted"))
        turned, copied0, copied1, mixed, scaled = (sem(n) for n in ("p_turned", "p_copied0", "p_copied1", "swa_mixed", "swa_scaled"))

        def cols(n):
            return slice(0 if n else WINDOW, 2 * WINDOW)

        with nc.Block() as block:
            @block.sync
            def _(sp):
                sp.dma_start(sink[:], swa_sinks.partition_broadcast(P)).then_inc(sinks_loaded, 16)

            @block.gpsimd
            def _(pool):
                nc.gpsimd.iota(rel[:], pattern=[[-1, 2 * WINDOW]], base=WINDOW, channel_multiplier=1,
                               allow_small_or_imprecise_dtypes=True).then_inc(rel_done, 1)
                for h in range(SWA_HEADS):
                    pool.wait_ge(sloped, h + 1)
                    nc.gpsimd.affine_select(out=bias[:, h, :], in_=bias[:, h, :], compare_op=ALU.is_ge, fill=-3e38, base=WINDOW,
                                            pattern=[[-1, 2 * WINDOW]], channel_multiplier=1).then_inc(bias_done, 1)
                    pool.wait_ge(bias_done, 2 * h + 1)
                    nc.gpsimd.affine_select(out=bias[:, h, :], in_=bias[:, h, :], compare_op=ALU.is_gt, fill=-3e38, base=0,
                                            pattern=[[1, 2 * WINDOW]], channel_multiplier=-1).then_inc(bias_done, 1)

            @block.tensor
            def _(pe):
                def scores(u):
                    n, g = units[u]
                    if u >= 2:
                        pe.wait_ge(biased, u - 1)
                    part = slice(g * DH, (g + 1) * DH)
                    k0 = max(n - 1, 0) * P
                    for h in range(GROUP):
                        last = nc.tensor.matmul(ps_s[u % 2][:, h, cols(n)], qbT[part, h, n * P:(n + 1) * P], kbT[part, 0, k0:(n + 1) * P],
                                                start=True, stop=True)
                    last.then_inc(scored, 1)

                def turn(u):
                    n, g = units[u]
                    pe.wait_ge(exped, GROUP * (u + 1))
                    for half in (0, 1):
                        if u:
                            pe.wait_ge(copied1 if half else copied0, u)
                        for h in range(GROUP):
                            if half or n:
                                last = nc.tensor.transpose(ps_t[half][:, h * P:(h + 1) * P], s[:, u % 2, h, half * P:(half + 1) * P], ident[:])
                        if half or n:
                            last.then_inc(turned, 1)
                        else:
                            pe.sem_inc(turned, 1)

                def mix(u):
                    n, g = units[u]
                    pe.wait_ge(copied0, u + 1)
                    pe.wait_ge(copied1, u + 1)
                    if u >= 2:
                        pe.wait_ge(scaled, u - 1)
                    for h in range(GROUP):
                        out = ps_o[u % 2][:, h * DH:(h + 1) * DH]
                        if n:
                            nc.tensor.matmul(out, pT[:, 0, h * P:(h + 1) * P], vbz[:, n - 1, g * DH:(g + 1) * DH], start=True, stop=False)
                        last = nc.tensor.matmul(out, pT[:, 1, h * P:(h + 1) * P], vbz[:, n, g * DH:(g + 1) * DH], start=(n == 0), stop=True)
                    last.then_inc(mixed, 1)

                scores(0)
                for u in range(len(units)):
                    if u + 1 < len(units):
                        scores(u + 1)
                    turn(u)
                    mix(u)

            @block.vector
            def _(dve):
                for h in range(SWA_HEADS):
                    dve.wait_ge(rel_done, 1)
                    nc.vector.tensor_scalar(bias[:, h, :], rel[:], -(2.0 ** (-8.0 * (h + 1) / SWA_HEADS)), None, ALU.mult).then_inc(sloped, 1)

                def scores(u):
                    n, g = units[u]
                    c, heads = cols(n), slice(g * GROUP, (g + 1) * GROUP)
                    dve.wait_ge(scored, u + 1)
                    if u >= 2:
                        dve.wait_ge(turned, 2 * (u - 1))
                    nc.vector.scalar_tensor_tensor(out=s[:, u % 2, :, c], in0=ps_s[u % 2][:, :, c], scalar=DH ** -0.5, in1=bias[:, heads, c],
                                                   op0=ALU.mult, op1=ALU.add).then_inc(biased, 1)
                    dve.wait_ge(biased, u + 1)
                    nc.vector.tensor_reduce(top[:, u % 2, :], s[:, u % 2, :, c], AX_X, ALU.max).then_inc(maxed, 1)
                    dve.wait_ge(maxed, u + 1)
                    nc.vector.tensor_tensor(top[:, u % 2, :], top[:, u % 2, :], sink[:, heads], ALU.max).then_inc(topped, 1)
                    dve.wait_ge(topped, u + 1)
                    nc.vector.tensor_scalar(low[:, u % 2, :], top[:, u % 2, :], -1.0, None, ALU.mult).then_inc(lowed, 1)
                    nc.vector.tensor_tensor(es[:, u % 2, :], sink[:, heads], top[:, u % 2, :], ALU.subtract).then_inc(sink_shifted, 1)

                def finish(u):
                    n, g = units[u]
                    dve.wait_ge(turned, 2 * u + 2)
                    if u:
                        dve.wait_ge(mixed, u)
                    nc.vector.tensor_copy(pT[:, 1, :], ps_t[1][:]).then_inc(copied1, 1)
                    dve.wait_ge(sink_exped, u + 1)
                    nc.vector.tensor_tensor(den[:, u % 2, :], den[:, u % 2, :], es[:, u % 2, :], ALU.add).then_inc(summed, 1)
                    dve.wait_ge(summed, u + 1)
                    nc.vector.reciprocal(den[:, u % 2, :], den[:, u % 2, :]).then_inc(inverted, 1)
                    dve.wait_ge(inverted, u + 1)
                    dve.wait_ge(mixed, u + 1)
                    nc.vector.tensor_tensor(cat[:, n, 512 + g * 256:512 + g * 256 + 256].rearrange("p (h c) -> p h c", c=DH),
                                            ps_o[u % 2][:, 0:256].rearrange("p (h c) -> p h c", c=DH),
                                            den[:, u % 2, :].unsqueeze(2).to_broadcast([P, GROUP, DH]), ALU.mult).then_inc(scaled, 1)

                dve.wait_ge(sinks_loaded, 16)
                dve.wait_ge(bias_done, 2 * SWA_HEADS)
                scores(0)
                for u in range(len(units)):
                    if u + 1 < len(units):
                        scores(u + 1)
                    finish(u)

            @block.scalar
            def _(act):
                def exps(u):
                    n, g = units[u]
                    c = cols(n)
                    act.wait_ge(lowed, u + 1)
                    if u >= 2:
                        act.wait_ge(scaled, u - 1)
                    for h in range(GROUP):
                        nc.scalar.activation(s[:, u % 2, h, c], s[:, u % 2, h, c], ACT.Exp, bias=low[:, u % 2, h:h + 1],
                                             accum_out=den[:, u % 2, h:h + 1]).then_inc(exped, 1)
                    act.wait_ge(sink_shifted, u + 1)
                    nc.scalar.activation(es[:, u % 2, :], es[:, u % 2, :], ACT.Exp).then_inc(sink_exped, 1)

                exps(0)
                for u in range(len(units)):
                    if u + 1 < len(units):
                        exps(u + 1)
                    act.wait_ge(turned, 2 * u + 1)
                    if u:
                        act.wait_ge(mixed, u)
                    if units[u][0]:
                        nc.scalar.activation(pT[:, 0, :], ps_t[0][:], ACT.Copy).then_inc(copied0, 1)
                    else:
                        act.sem_inc(copied0, 1)


def mix_out(nc, x, w_out, gla_norm_g, swa_norm_g, norm2_g, w_router, b_router, ident, ra, cat, logits, h_rows, hn_rows):
    GG = GLA_HEADS + SWA_HEADS
    with ExitStack() as ctx:
        def sb(name, shape, dt=F32):
            return ctx.enter_context(nc.sbuf_tensor(name, shape, dt))

        def sem(name):
            return ctx.enter_context(nc.semaphore(name))

        raw = sb("w_out_raw", [P, 2, D])
        wh, wl = sb("w_out_hi", [P, KT, D], F32R), sb("w_out_lo", [P, KT, D], F32R)
        gains = sb("head_gains", [P, D])
        g2 = sb("norm2_rows", [P, D])
        w_r, b_r = sb("w_router", [P, KT, EXPERTS]), sb("b_router", [P, EXPERTS])
        xt, ht = sb("x_again", [P, D]), sb("h_tile", [P, D])
        hn = sb("hn_tile", [P, D])
        cTh, cTl = sb("catT_hi", [P, KT, P], F32R), sb("catT_lo", [P, KT, P], F32R)
        hnT = sb("hnT", [P, KT, P])
        ss, rms, rstd = (sb(n, [P, GG]) for n in ("head_ss", "head_rms", "head_rstd"))
        ss2, rms2, rstd2 = (sb(n, [P, TILES]) for n in ("h_ss", "h_rms", "h_rstd"))
        eps, eps_g = sb("eps2", [P, 1]), sb("eps_gla", [P, 1])
        sq = sb("squares", [P, D])
        ps_t = [ctx.enter_context(nc.psum_tensor(f"out_t{i}", [P, 512], F32)) for i in range(2)]
        ps_h = [ctx.enter_context(nc.psum_tensor(f"out_h{i}", [P, D], F32)) for i in range(2)]
        ps_l = ctx.enter_context(nc.psum_tensor("out_logits", [P, 512], F32))

        gains_loaded, g2_loaded, router_loaded, eps_set = sem("gains_loaded"), sem("g2_loaded"), sem("router_loaded"), sem("eps2_set")
        w_loaded, w_hi, w_lo = [sem(f"w_out_loaded{i}") for i in range(2)], sem("w_out_hi_s"), sem("w_out_lo_s")
        x_loaded = sem("x_again_loaded")
        sig_done, silu_done = sem("sig_done"), sem("silu_done")
        squared, grouped, rooted, inverted = sem("squared"), sem("grouped"), sem("head_rooted"), sem("head_inverted")
        scaled, gained, gated = sem("head_scaled"), sem("head_gained"), sem("head_gated")
        turned, t_hi, t_lo = sem("cat_turned"), sem("catT_hi_s"), sem("catT_lo_s")
        h_ready, h_added, h_squared, h_rooted, h_inverted = sem("h_ready"), sem("h_added"), sem("h_squared"), sem("h_rooted"), sem("h_inverted")
        hn_done, hn_turned, hnT_done, logit_ready, logit_done = sem("hn_done"), sem("hn_turned"), sem("hnT_done"), sem("logit_ready"), sem("logit_done")
        h_stored, hn_stored = sem("h_stored"), sem("hn_stored")

        w_rows = w_out.rearrange("(k p) n -> k p n", p=P)
        x_t, h_t, hn_t = (a.rearrange("(t p) d -> t p d", p=P) for a in (x, h_rows, hn_rows))

        with nc.Block() as block:
            @block.sync
            def _(sp):
                for k in range(KT):
                    if k >= 2:
                        sp.wait_ge(w_lo, k - 1)
                    sp.dma_start(raw[:, k % 2, :], w_rows[k]).then_inc(w_loaded[k % 2], 16)
                for t in range(TILES):
                    if t:
                        sp.wait_ge(h_added, 2 * t)
                    sp.dma_start(xt[:], x_t[t]).then_inc(x_loaded, 16)
                    sp.wait_ge(hn_done, t + 1)
                    sp.dma_start(h_t[t], ht[:]).then_inc(h_stored, 16)
                    sp.dma_start(hn_t[t], hn[:]).then_inc(hn_stored, 16)
                sp.wait_ge(h_stored, 16 * TILES)
                sp.wait_ge(hn_stored, 16 * TILES)

            def hnT_as(t):
                return hnT[:].rearrange("p k n -> p (k n)")[:, t % 2 * 512:t % 2 * 512 + 512]

            @block.gpsimd
            def _(pool):
                for h in range(GLA_HEADS):
                    pool.dma_start(gains[:, h * GLA_DV:(h + 1) * GLA_DV], gla_norm_g.partition_broadcast(P)).then_inc(gains_loaded, 16)
                for h in range(SWA_HEADS):
                    pool.dma_start(gains[:, 512 + h * DH:512 + (h + 1) * DH], swa_norm_g.partition_broadcast(P)).then_inc(gains_loaded, 16)
                pool.dma_start(g2[:], norm2_g.partition_broadcast(P)).then_inc(g2_loaded, 16)
                pool.dma_start(w_r[:], w_router.rearrange("(k p) e -> p k e", p=P)).then_inc(router_loaded, 16)
                pool.dma_start(b_r[:], b_router.partition_broadcast(P)).then_inc(router_loaded, 16)
                for t in range(TILES):
                    pool.wait_ge(sig_done, t + 1)
                    nc.gpsimd.tensor_tensor(ra[:, t, :], ra[:, t, :], hnT_as(t), ALU.mult).then_inc(silu_done, 1)

            @block.scalar
            def _(act):
                for t in range(TILES):
                    if t >= 2:
                        act.wait_ge(silu_done, t - 1)
                    nc.scalar.activation(hnT_as(t), ra[:, t, :], ACT.Sigmoid).then_inc(sig_done, 1)
                act.wait_ge(eps_set, 1)
                for k in range(KT):
                    act.wait_ge(w_loaded[k % 2], 16 * (k // 2 + 1))
                    nc.scalar.activation(wh[:, k, :], raw[:, k % 2, :], ACT.Copy).then_inc(w_hi, 1)

                def root(t):
                    if t:
                        act.wait_ge(grouped, 2 * t)
                    nc.scalar.activation(sq[:], cat[:, t, :], ACT.Square).then_inc(squared, 1)
                    act.wait_ge(grouped, 2 * t + 2)
                    if t:
                        act.wait_ge(inverted, t)
                    nc.scalar.activation(rms[:, 0:GLA_HEADS], ss[:, 0:GLA_HEADS], ACT.Sqrt, bias=eps[:], scale=1.0 / GLA_DV).then_inc(rooted, 1)
                    nc.scalar.activation(rms[:, GLA_HEADS:GG], ss[:, GLA_HEADS:GG], ACT.Sqrt, bias=eps[:], scale=1.0 / DH).then_inc(rooted, 1)

                def turn(t):
                    for half in range(2):
                        act.wait_ge(turned, 2 * t + half + 1)
                        if t:
                            act.wait_ge(h_ready, t)
                        nc.scalar.activation(cTh[:, half * 4:half * 4 + 4, :], ps_t[half][:].rearrange("p (k n) -> p k n", k=4),
                                             ACT.Copy).then_inc(t_hi, 1)

                root(0)
                turn(0)
                for t in range(TILES):
                    if t + 1 < TILES:
                        root(t + 1)
                        turn(t + 1)
                    act.wait_ge(h_added, 2 * t + 2)
                    if t:
                        act.wait_ge(hn_stored, 16 * t)
                        act.wait_ge(hn_turned, 2 * t)
                    nc.scalar.activation(hn[:], ht[:], ACT.Square, accum_out=ss2[:, t:t + 1]).then_inc(h_squared, 1)
                    act.wait_ge(h_squared, t + 1)
                    nc.scalar.activation(rms2[:, t:t + 1], ss2[:, t:t + 1], ACT.Sqrt, bias=eps[:], scale=1.0 / D).then_inc(h_rooted, 1)
                    for half in range(2):
                        act.wait_ge(hn_turned, 2 * t + half + 1)
                        if t:
                            act.wait_ge(logit_ready, t)
                        else:
                            act.wait_ge(silu_done, TILES)
                        nc.scalar.activation(hnT[:, half * 4:half * 4 + 4, :], ps_t[half][:].rearrange("p (k n) -> p k n", k=4),
                                             ACT.Copy).then_inc(hnT_done, 1)

            @block.vector
            def _(dve):
                nc.vector.memset(eps[:], EPS).then_inc(eps_set, 1)
                dve.wait_ge(gains_loaded, 16 * GG)
                for k in range(KT):
                    dve.wait_ge(w_hi, k + 1)
                    nc.vector.tensor_tensor(wl[:, k, :], raw[:, k % 2, :], wh[:, k, :].bitcast(F32), ALU.subtract).then_inc(w_lo, 1)

                def norm(t):
                    dve.wait_ge(squared, t + 1)
                    if t:
                        dve.wait_ge(rooted, 2 * t)
                    nc.vector.reduce_sum(ss[:, 0:GLA_HEADS], sq[:, 0:512].rearrange("p (h v) -> p h v", v=GLA_DV), AX_X).then_inc(grouped, 1)
                    nc.vector.reduce_sum(ss[:, GLA_HEADS:GG], sq[:, 512:D].rearrange("p (h v) -> p h v", v=DH), AX_X).then_inc(grouped, 1)
                    dve.wait_ge(rooted, 2 * t + 2)
                    if t:
                        dve.wait_ge(scaled, 2 * t)
                    nc.vector.reciprocal(rstd[:], rms[:]).then_inc(inverted, 1)
                    dve.wait_ge(inverted, t + 1)
                    a = cat[:, t, 0:512].rearrange("p (h v) -> p h v", v=GLA_DV)
                    b = cat[:, t, 512:D].rearrange("p (h v) -> p h v", v=DH)
                    nc.vector.tensor_tensor(a, a, rstd[:, 0:GLA_HEADS].unsqueeze(2).to_broadcast([P, GLA_HEADS, GLA_DV]), ALU.mult).then_inc(scaled, 1)
                    nc.vector.tensor_tensor(b, b, rstd[:, GLA_HEADS:GG].unsqueeze(2).to_broadcast([P, SWA_HEADS, DH]), ALU.mult).then_inc(scaled, 1)
                    dve.wait_ge(scaled, 2 * t + 2)
                    nc.vector.tensor_tensor(cat[:, t, :], cat[:, t, :], gains[:], ALU.mult).then_inc(gained, 1)
                    dve.wait_ge(gained, t + 1)
                    dve.wait_ge(silu_done, t + 1)
                    nc.vector.tensor_tensor(cat[:, t, 0:512], cat[:, t, 0:512], ra[:, t, :], ALU.mult).then_inc(gated, 1)

                def turn(t):
                    for half in range(2):
                        dve.wait_ge(t_hi, 2 * t + half + 1)
                        nc.vector.tensor_tensor(cTl[:, half * 4:half * 4 + 4, :], ps_t[half][:].rearrange("p (k n) -> p k n", k=4),
                                                cTh[:, half * 4:half * 4 + 4, :].bitcast(F32), ALU.subtract).then_inc(t_lo, 1)

                norm(0)
                turn(0)
                dve.wait_ge(g2_loaded, 16)
                dve.wait_ge(router_loaded, 32)
                for t in range(TILES):
                    if t + 1 < TILES:
                        norm(t + 1)
                        turn(t + 1)
                    dve.wait_ge(h_ready, t + 1)
                    dve.wait_ge(x_loaded, 16 * (t + 1))
                    if t:
                        dve.wait_ge(h_stored, 16 * t)
                    for half in range(2):
                        c = slice(half * 512, half * 512 + 512)
                        nc.vector.tensor_tensor(ht[:, c], ps_h[t % 2][:, c], xt[:, c], ALU.add).then_inc(h_added, 1)
                    dve.wait_ge(h_rooted, t + 1)
                    nc.vector.reciprocal(rstd2[:, t:t + 1], rms2[:, t:t + 1]).then_inc(h_inverted, 1)
                    dve.wait_ge(h_inverted, t + 1)
                    nc.vector.scalar_tensor_tensor(out=hn[:], in0=ht[:], scalar=rstd2[:, t:t + 1], in1=g2[:],
                                                   op0=ALU.mult, op1=ALU.mult).then_inc(hn_done, 1)
                    dve.wait_ge(logit_ready, t + 1)
                    nc.vector.tensor_tensor(logits[:, t, :], ps_l[:, 0:EXPERTS], b_r[:], ALU.add).then_inc(logit_done, 1)

            @block.tensor
            def _(pe):
                def turn(t):
                    pe.wait_ge(gated, t + 1)
                    for half in range(2):
                        if t == 1:
                            pe.wait_ge(t_lo, half + 1)
                        elif t:
                            pe.wait_ge(hnT_done, 2 * (t - 2) + half + 1)
                        for k in range(4):
                            c = (half * 4 + k) * P
                            last = nc.tensor.transpose(ps_t[half][:, k * P:(k + 1) * P], cat[:, t, c:c + P], ident[:])
                        last.then_inc(turned, 1)

                turn(0)
                for t in range(TILES):
                    pe.wait_ge(t_lo, 2 * t + 2)
                    if t >= 2:
                        pe.wait_ge(h_added, 2 * (t - 1))
                    for k in range(KT):
                        if t == 0:
                            pe.wait_ge(w_lo, k + 1)
                        for half in range(2):
                            c = slice(half * 512, half * 512 + 512)
                            out = ps_h[t % 2][:, c]
                            nc.tensor.matmul(out, cTh[:, k, :], wh[:, k, c], start=(k == 0), stop=False)
                            nc.tensor.matmul(out, cTh[:, k, :], wl[:, k, c], start=False, stop=False)
                            mm = nc.tensor.matmul(out, cTl[:, k, :], wh[:, k, c], start=False, stop=(k == KT - 1))
                    mm.then_inc(h_ready, 1)
                    if t + 1 < TILES:
                        turn(t + 1)
                    pe.wait_ge(hn_done, t + 1)
                    for half in range(2):
                        if t + 1 < TILES:
                            pe.wait_ge(t_lo, 2 * (t + 1) + half + 1)
                        for k in range(4):
                            c = (half * 4 + k) * P
                            last = nc.tensor.transpose(ps_t[half][:, k * P:(k + 1) * P], hn[:, c:c + P], ident[:])
                        last.then_inc(hn_turned, 1)
                    pe.wait_ge(hnT_done, 2 * t + 2)
                    if t:
                        pe.wait_ge(logit_done, t)
                    for k in range(KT):
                        mm = nc.tensor.matmul(ps_l[:, 0:EXPERTS], hnT[:, k, :], w_r[:, k, :], start=(k == 0), stop=(k == KT - 1))
                    mm.then_inc(logit_ready, 1)


def dispatch(nc, logits, gate, token_of, pair_of, group_expert, group_second, last_group):
    E, T = EXPERTS, TILES
    with ExitStack() as ctx:
        def sb(name, shape, dt=F32):
            return ctx.enter_context(nc.sbuf_tensor(name, shape, dt))

        def sem(name):
            return ctx.enter_context(nc.semaphore(name))

        best, where, where_f = sb("best", [P, T, 8]), sb("where", [P, T, 8], U32), sb("where_f", [P, T, 8])
        shifted, total = sb("gate_shifted", [P, T, TOP_K]), sb("gate_total", [P, T])
        e_iota, row_iota, pair_iota = sb("e_iota", [P, T, E]), sb("row_iota", [P, P]), sb("pair_iota", [P, TOP_K, T])
        spare_iota = sb("spare_iota", [P, BLOCKS])
        empty, pair_i = sb("row_empty", [P, BLOCKS]), sb("pair_i", [P, BLOCKS], I32)
        g_iota = sb("g_iota", [1, GROUPS, E])
        hot, mask, place, tmp = sb("hot", [P, TOP_K, T, E]), sb("routed", [P, T, E]), sb("place", [P, T, E]), sb("place_k", [P, TOP_K, T, E])
        below, ones = sb("below", [P, P]), sb("all_ones", [P, P])
        before = sb("tiles_before", [P, T + 1, E])
        ints, halves = sb("count_i", [P, E], I32), sb("half_i", [P, E], I32)
        n_groups, ends, starts, pairs_of_blocks = (sb(n, [P, E]) for n in ("n_groups", "group_ends", "group_starts", "full_groups"))
        dest_f, dest_i, low_f, block_f = sb("dest_f", [P, TOP_K, T]), sb("dest_i", [P, TOP_K, T], I32), sb("low_f", [P, TOP_K, T]), sb("block_f", [P, TOP_K, T])
        low_i = sb("low_i", [P, TOP_K, T], I32)
        J, R = sb("row_hot", [P, 4, P]), sb("block_hot", [P, 4, BLOCKS])
        cmp1, cmp2 = sb("cmp1", [1, GROUPS, E]), sb("cmp2", [1, GROUPS, E])
        row1, row2 = sb("row1", [1, GROUPS]), sb("row2", [1, GROUPS])
        ps_p = ctx.enter_context(nc.psum_tensor("place_ps", [P, 512], F32))
        ps_c = ctx.enter_context(nc.psum_tensor("count_ps", [P, 512], F32))
        ps_tok = ctx.enter_context(nc.psum_tensor("token_ps", [P, 512], F32))

        step, made, made0 = sem("dve_step"), sem("consts_made"), sem("ones_made")
        masked, prefixed = sem("routed_s"), sem("prefixed")
        gates_in, gates_exp = sem("gates_in"), sem("gates_exp")
        hot_ready, hot_used, tokens_ready = sem("hot_ready"), sem("hot_used"), sem("tokens_ready")

        with nc.Block() as block:
            @block.gpsimd
            def _(pool):
                nc.gpsimd.memset(ones[:], 1.0).then_inc(made0, 1)
                pool.wait_ge(made0, 1)
                nc.gpsimd.affine_select(out=below[:], in_=ones[:], compare_op=ALU.is_gt, fill=0.0, base=0,
                                        pattern=[[1, P]], channel_multiplier=-1).then_inc(made, 1)
                pairs_plus_1, spare_plus_1 = pair_iota[:], spare_iota[:]
                for ap, pattern, mult in ((e_iota[:], [[0, T], [1, E]], 0), (row_iota[:], [[1, P]], 0), (pairs_plus_1, [[1, TOP_K], [TOP_K * P, T]], TOP_K),
                                          (g_iota[:], [[1, GROUPS], [0, E]], 0), (spare_plus_1, [[0, GROUPS], [P, 2]], 1)):
                    base = 1 if ap is pairs_plus_1 else SPARE + 1 if ap is spare_plus_1 else 0
                    nc.gpsimd.iota(ap, pattern=pattern, base=base, channel_multiplier=mult, allow_small_or_imprecise_dtypes=True).then_inc(made, 1)

            @block.scalar
            def _(act):
                act.wait_ge(gates_in, 1)
                nc.scalar.activation(shifted[:], shifted[:], ACT.Exp).then_inc(gates_exp, 1)

            @block.vector
            def _(dve):
                count = [0]

                def then(ins):
                    count[0] += 1
                    ins.then_inc(step, 1)
                    dve.wait_ge(step, count[0])

                v = nc.vector
                for t in range(T):
                    v.max(best[:, t, :], logits[:, t, :]).then_inc(step, 1)
                count[0] += T
                dve.wait_ge(step, count[0])
                for t in range(T):
                    v.max_index(where[:, t, :], best[:, t, :], logits[:, t, :]).then_inc(step, 1)
                count[0] += T
                dve.wait_ge(step, count[0])
                v.tensor_tensor(shifted[:], best[:, :, 0:TOP_K], best[:, :, 0:1].to_broadcast([P, T, TOP_K]), ALU.subtract).then_inc(gates_in, 1)
                then(v.tensor_copy(where_f[:], where[:]))
                dve.wait_ge(made, 6)
                for k in range(TOP_K):
                    v.tensor_tensor(hot[:, k], e_iota[:], where_f[:, :, k:k + 1].to_broadcast([P, T, E]), ALU.is_equal).then_inc(step, 1)
                count[0] += TOP_K
                dve.wait_ge(step, count[0])
                then(v.tensor_tensor(mask[:], hot[:, 0], hot[:, 1], ALU.add))
                then(v.tensor_tensor(mask[:], mask[:], hot[:, 2], ALU.add))
                v.tensor_tensor(mask[:], mask[:], hot[:, 3], ALU.add).then_inc(masked, 1)
                dve.wait_ge(gates_exp, 1)
                then(v.reduce_sum(total[:], shifted[:], AX_X))
                then(v.reciprocal(total[:], total[:]))
                then(v.tensor_tensor(gate[:], shifted[:], total[:].unsqueeze(2).to_broadcast([P, T, TOP_K]), ALU.mult))
                dve.wait_ge(prefixed, 2)
                then(v.memset(before[:, 0, :], 0.0))
                for t in range(T):
                    then(v.tensor_tensor(before[:, t + 1, :], before[:, t, :], ps_c[:, t * E:(t + 1) * E], ALU.add))
                then(v.tensor_tensor(place[:], ps_p[:, 0:T * E].rearrange("p (t e) -> p t e", t=T), before[:, 0:T, :], ALU.add))
                then(v.tensor_scalar(ints[:], before[:, T, :], float(GROUP_ROWS - 1), None, ALU.add))
                then(v.tensor_scalar(ints[:], ints[:], 8, None, ALU.arith_shift_right))
                then(v.tensor_copy(n_groups[:], ints[:]))
                then(v.tensor_scalar(halves[:], before[:, T, :], float(P - 1), None, ALU.add))
                then(v.tensor_scalar(halves[:], halves[:], 8, None, ALU.arith_shift_right))
                then(v.tensor_copy(pairs_of_blocks[:], halves[:]))
                then(v.tensor_tensor_scan(ends[:], ones[:, 0:E], n_groups[:], 0.0, ALU.mult, ALU.add))
                then(v.tensor_tensor(starts[:], ends[:], n_groups[:], ALU.subtract))
                then(v.tensor_scalar(n_groups[:], starts[:], float(GROUP_ROWS), None, ALU.mult))
                then(v.tensor_tensor(place[:], place[:], n_groups[:].unsqueeze(1).to_broadcast([P, T, E]), ALU.add))
                for k in range(TOP_K):
                    v.tensor_tensor(tmp[:, k], hot[:, k], place[:], ALU.mult).then_inc(step, 1)
                count[0] += TOP_K
                dve.wait_ge(step, count[0])
                then(v.reduce_sum(dest_f[:].rearrange("p k t -> p (k t)"), tmp[:].rearrange("p k t e -> p (k t) e"), AX_X))
                then(v.tensor_copy(dest_i[:], dest_f[:]))
                then(v.tensor_scalar(low_i[:], dest_i[:], P - 1, None, ALU.bitwise_and))
                then(v.tensor_scalar(dest_i[:], dest_i[:], 7, None, ALU.arith_shift_right))
                then(v.tensor_copy(low_f[:], low_i[:]))
                then(v.tensor_copy(block_f[:], dest_i[:]))
                for n in range(TOP_K * T):
                    k, t = n // T, n % T
                    if n >= 4:
                        dve.wait_ge(hot_used, n - 3)
                    v.tensor_scalar(J[:, n % 4, :], row_iota[:], low_f[:, k, t:t + 1], None, ALU.is_equal).then_inc(hot_ready, 1)
                    v.tensor_scalar(R[:, n % 4, :], row_iota[:, 0:BLOCKS], block_f[:, k, t:t + 1], pair_iota[:, k, t:t + 1],
                                    ALU.is_equal, ALU.mult).then_inc(hot_ready, 1)
                end_row, start_row, full_row = (a[0:1, :].unsqueeze(1).to_broadcast([1, GROUPS, E]) for a in (ends, starts, pairs_of_blocks))
                then(v.tensor_tensor(cmp1[:], g_iota[:], end_row, ALU.is_ge))
                then(v.reduce_sum(row1[:], cmp1[:], AX_X))
                then(v.tensor_scalar(row1[:], row1[:], float(E - 1), None, ALU.min))
                then(v.tensor_copy(group_expert[:], row1[:]))
                then(v.tensor_tensor(cmp1[:], g_iota[:], start_row, ALU.subtract))
                then(v.tensor_tensor(cmp2[:], cmp1[:], full_row, ALU.is_lt))
                then(v.tensor_scalar(cmp1[:], cmp1[:], 0.0, None, ALU.is_ge))
                then(v.tensor_tensor(cmp1[:], cmp1[:], cmp2[:], ALU.mult))
                then(v.reduce_sum(row2[:], cmp1[:], AX_X))
                then(v.tensor_copy(group_second[:], row2[:]))
                then(v.tensor_scalar(last_group[:], ends[0:1, E - 1:E], -1.0, None, ALU.add))
                dve.wait_ge(tokens_ready, 1)
                then(v.tensor_scalar(empty[:], ps_tok[:, 0:BLOCKS], 0.0, None, ALU.is_equal))
                then(v.tensor_tensor(empty[:], empty[:], spare_iota[:], ALU.mult))
                then(v.tensor_tensor(empty[:], ps_tok[:, 0:BLOCKS], empty[:], ALU.add))
                then(v.tensor_scalar(pair_i[:], empty[:], -1.0, None, ALU.add))
                then(v.tensor_copy(pair_of[:], pair_i[:]))
                then(v.tensor_scalar(pair_i[:], empty[:], -1.0, float(TOP_K * SEQ - 1), ALU.add, ALU.min))
                then(v.tensor_scalar(pair_i[:], pair_i[:], 2, None, ALU.arith_shift_right))
                then(v.tensor_copy(token_of[:], pair_i[:]))

            @block.tensor
            def _(pe):
                pe.wait_ge(masked, 1)
                pe.wait_ge(made, 1)
                rows = mask[:].rearrange("p t e -> p (t e)")
                nc.tensor.matmul(ps_p[:, 0:T * E], below[:], rows, start=True, stop=True).then_inc(prefixed, 1)
                nc.tensor.matmul(ps_c[:, 0:T * E], ones[:], rows, start=True, stop=True).then_inc(prefixed, 1)
                for n in range(TOP_K * T):
                    pe.wait_ge(hot_ready, 2 * n + 2)
                    mm = nc.tensor.matmul(ps_tok[:, 0:BLOCKS], J[:, n % 4, :], R[:, n % 4, :], start=(n == 0), stop=(n == TOP_K * T - 1))
                    mm.then_inc(hot_used, 1)
                pe.wait_ge(hot_used, TOP_K * T)
                pe.sem_inc(tokens_ready, 1)


def experts(nc, hn_rows, w_glu, b_glu, w_lin, b_lin, w_down, b_down, ident, token_of, group_expert, group_second, last_group, pair_of, y_rows):
    SLOTS = 4
    LEAD = SLOTS - 1
    UP, TURN = 8, 12
    BANKS = 3
    with ExitStack() as ctx:
        def sb(name, shape, dt=F32):
            return ctx.enter_context(nc.sbuf_tensor(name, shape, dt))

        def sem(name):
            return ctx.enter_context(nc.semaphore(name))

        raw = sb("w_raw", [P, SLOTS, 4, 512])
        wh, wl = sb("w_hi", [P, SLOTS, 4, 512], F32R), sb("w_lo", [P, SLOTS, 4, 512], F32R)
        rows = sb("group_rows", [P, 2, D])
        xTh, xTl = sb("xT_hi", [P, 2, KT, P], F32R), sb("xT_lo", [P, 2, KT, P], F32R)
        hTh, hTl = sb("hidT_hi", [P, 2, KT, P], F32R), sb("hidT_lo", [P, 2, KT, P], F32R)
        glu, sig, lin = sb("glu", [P, 2, DFF]), sb("glu_sigmoid", [P, 2, 512]), sb("lin", [P, 2, 512])
        hid = sb("hidden", [P, 2, DFF])
        y = sb("y", [P, 2, D])
        bias_g, bias_l, bias_d = sb("glu_bias", [P, DFF]), sb("lin_bias", [P, DFF]), sb("down_bias", [P, D])
        ps_t = [ctx.enter_context(nc.psum_tensor(f"piece_ps{i}", [P, 512], F32)) for i in range(2)]
        ps_u = [ctx.enter_context(nc.psum_tensor(f"unit_ps{i}", [P, 2, 512], F32)) for i in range(BANKS)]

        w_loaded = [sem(f"w_loaded{i}") for i in range(SLOTS)]
        w_hi, w_lo, half_done = sem("w_hi_s"), sem("w_lo_s"), sem("half_done")
        unit_taken = sem("unit_taken")
        rows_loaded = [sem(f"rows_loaded{i}") for i in range(2)]
        turned, piece_hi, piece_lo = sem("piece_turned"), sem("piece_hi"), sem("piece_lo")
        up_bias_loaded, down_bias_loaded = sem("up_bias_loaded"), sem("down_bias_loaded")
        clipped, sig_done, swished = sem("glu_clipped"), sem("glu_sig_done"), sem("glu_swished")
        lin_clipped, hid_done = sem("lin_clipped"), sem("hid_done")
        act_ended, gather_begun = sem("act_ended"), sem("gather_begun")
        y_done, y_stored = sem("y_done"), sem("y_stored")
        y_free = sem("y_free")

        mats = [m.rearrange("e (k p) n -> e p k n", p=P) for m in (w_glu, w_lin, w_down)]

        def halves_before(s):
            return TURN * s - (TURN - UP)

        def units_before(s):
            return 6 * s - 2

        def unit_bank(n):
            return (n - 2) % BANKS

        def groups_of(eng):
            return eng.value_load(last_group[0:1, 0:1], min_val=TOP_K * SEQ // GROUP_ROWS - 1, max_val=MAX_GROUPS - 1) + 1

        def expert_at(eng, s):
            return eng.value_load(group_expert[0:1, bass.ds(s, 1)], min_val=0, max_val=EXPERTS - 1)

        def second_at(eng, s):
            return eng.value_load(group_second[0:1, bass.ds(s, 1)], min_val=0, max_val=1)

        def for_blocks(eng, second, emit):
            with eng.If(second == 1):
                emit(2)
            with eng.Else():
                emit(1)

        with nc.Block() as block:
            @block.sync
            def _(sp):
                count = groups_of(sp)

                def load(matrix, expert, column_half, k_half, slot, before):
                    if before is not None:
                        sp.wait_ge(w_lo, before)
                    sp.dma_start(raw[:, slot], mats[matrix][bass.ds(expert, 1), :, k_half * 4:k_half * 4 + 4, column_half * 512:column_half * 512 + 512]
                                 .rearrange("e p k n -> p (e k) n")).then_inc(w_loaded[slot], 16)

                def load_up(s, base):
                    expert = expert_at(sp, s)
                    for i in range(UP):
                        free = base + i - SLOTS + 1
                        load(i // 4, expert, i // 2 % 2, i % 2, i % SLOTS, free if not isinstance(free, int) or free > 0 else None)

                def load_down(s, base):
                    expert = expert_at(sp, s)
                    for i in range(TURN - UP):
                        load(2, expert, i // 2, i % 2, i % SLOTS, base + i - SLOTS + 1)

                load_up(0, 0)
                with sp.Fori(1, count) as s:
                    load_up(s, halves_before(s))
                    load_down(s - 1, halves_before(s) + UP)
                load_down(count - 1, halves_before(count))

            @block.gpsimd
            def _(pool):
                count = groups_of(pool)

                def gather(s):
                    def fetch(j):
                        pool.indirect_dma_start(rows[:, j, :], None, hn_rows, bass.IndirectOffsetOnAxis(ap=indices[:, j:j + 1], axis=0)
                                                ).then_inc(rows_loaded[j], 16)
                    nc.gpsimd.tensor_copy(indices[:], token_of[:, bass.ds(s * 2, 2)]).then_inc(index_ready, 1)
                    pool.wait_ge(index_ready, s + 1)
                    pool.sem_inc(gather_begun, 1)
                    fetch(0)
                    fetch(1)

                def store(s):
                    nc.gpsimd.tensor_copy(places[:], pair_of[:, bass.ds(s * 2, 2)]).then_inc(place_ready, 1)
                    pool.wait_ge(place_ready, s + 1)
                    pool.wait_ge(y_done, 2 * s + 4)
                    pool.sem_inc(gather_begun, 1)
                    for j in (0, 1):
                        pool.indirect_dma_start(y_rows, bass.IndirectOffsetOnAxis(ap=places[:, j:j + 1], axis=0), y[:, j, :], None
                                                ).then_inc(y_stored, 16)
                    pool.wait_ge(y_stored, 32 * (s + 1))
                    pool.sem_inc(y_free, 1)

                places, place_ready, y_zeroed = sb("row_pairs", [P, 2], U32), sem("place_ready"), sem("y_zeroed")
                nc.gpsimd.memset(y[:], 0.0).then_inc(y_zeroed, 1)
                pool.wait_ge(y_zeroed, 1)
                indices, index_ready = sb("row_tokens", [P, 2], U32), sem("index_ready")
                pool.sem_inc(y_free, 1)
                gather(0)
                pool.wait_ge(turned, 4)
                gather(1)
                with pool.Fori(1, count) as s:
                    pool.wait_ge(turned, 8 * s)
                    gather(s + 1)
                    store(s - 1)
                store(count - 1)

            @block.scalar
            def _(act):
                count = groups_of(act)

                def split(n, base, offset):
                    slot = n % SLOTS
                    act.wait_ge(w_loaded[slot], (base // SLOTS if isinstance(base, int) else offset) * 16 + 16 * (n // SLOTS + 1))
                    if not isinstance(base, int) or base + n >= SLOTS:
                        act.wait_ge(half_done, base + n - SLOTS + 1)
                    nc.scalar.activation(wh[:, slot], raw[:, slot], ACT.Copy).then_inc(w_hi, 1)

                def sigmoid(s, c, nb, turns):
                    act.wait_ge(clipped, 2 * s + c + 1)
                    if turns or c:
                        act.wait_ge(swished, 2 * s + c)
                    nc.scalar.activation(sig[:, 0:nb], glu[:, 0:nb, c * 512:c * 512 + 512], ACT.Sigmoid, scale=ALPHA).then_inc(sig_done, 1)

                def piece(n, to, j, q):
                    act.wait_ge(turned, n + 1)
                    nc.scalar.activation(to[:, j, 4 * q:4 * q + 4, :], ps_t[q][:].rearrange("p (k n) -> p k n", k=4), ACT.Copy).then_inc(piece_hi, 1)

                def pieces2(n, to, second, q):
                    with act.If(second == 1):
                        piece(n, to, 1, q)
                    with act.Else():
                        act.wait_ge(piece_hi, n)
                        act.sem_inc(piece_hi, 1)

                def load_up_bias(s):
                    expert = expert_at(act, s)
                    for to, of in ((bias_g, b_glu), (bias_l, b_lin)):
                        act.dma_start(to[:], of[bass.ds(expert, 1), :].to_broadcast([P, DFF])).then_inc(up_bias_loaded, 16)

                def turn(s, first):
                    base = 0 if first else halves_before(s)
                    offset = None if first else 3 * s - 1
                    second, second_next = second_at(act, s), second_at(act, s + 1)
                    if not first:
                        second_last, last_expert = second_at(act, s - 1), expert_at(act, s - 1)
                    P0 = 4 if first else 8 * s
                    for i in range(UP if first else TURN):
                        if i == 1 and not first:
                            act.wait_ge(y_done, 2 * s)
                            act.dma_start(bias_d[:], b_down[bass.ds(last_expert, 1), :].to_broadcast([P, D])).then_inc(down_bias_loaded, 16)
                        if i in (3, 5):
                            for_blocks(act, second, lambda nb: sigmoid(s, (i - 3) // 2, nb, not first))
                        if not first:
                            if i in (2, 3):
                                piece(P0 + i - 2, hTh, 0, i - 2)
                            if i in (4, 5):
                                pieces2(P0 + i - 2, hTh, second_last, i - 4)
                            if i in (8, 9):
                                piece(P0 + i - 4, xTh, 0, i - 8)
                            if i in (10, 11):
                                pieces2(P0 + i - 4, xTh, second_next, i - 10)
                        if i == 9:
                            act.wait_ge(hid_done, 2 * s + 2)
                            load_up_bias(s + 1)
                        split(i + LEAD, base, offset)
                    if first:
                        for q in (0, 1):
                            piece(P0 + q, xTh, 0, q)
                        for q in (0, 1):
                            pieces2(P0 + 2 + q, xTh, second_next, q)
                        act.wait_ge(hid_done, 2)
                        load_up_bias(1)

                load_up_bias(0)
                second = second_at(act, 0)
                for q in (0, 1):
                    piece(q, xTh, 0, q)
                for q in (0, 1):
                    pieces2(2 + q, xTh, second, q)
                for h in range(LEAD):
                    split(h, 0, None)
                turn(0, True)
                with act.Fori(1, count) as s:
                    turn(s, False)
                last, expert = second_at(act, count - 1), expert_at(act, count - 1)
                act.wait_ge(y_done, 2 * count)
                act.dma_start(bias_d[:], b_down[bass.ds(expert, 1), :].to_broadcast([P, D])).then_inc(down_bias_loaded, 16)
                for q in (0, 1):
                    piece(8 * count + q, hTh, 0, q)
                for q in (0, 1):
                    pieces2(8 * count + 2 + q, hTh, last, q)
                split(LEAD, halves_before(count), 3 * count - 1)
                act.wait_ge(up_bias_loaded, 32 * (count + 1))
                act.wait_ge(down_bias_loaded, 16 * count)
                act.sem_inc(act_ended, 1)

            @block.vector
            def _(dve):
                count = groups_of(dve)
                v = nc.vector

                def split(n, base):
                    slot = n % SLOTS
                    dve.wait_ge(w_hi, base + n + 1)
                    if not isinstance(base, int) or base + n >= SLOTS:
                        dve.wait_ge(half_done, base + n - SLOTS + 1)
                    v.tensor_tensor(wl[:, slot], raw[:, slot], wh[:, slot].bitcast(F32), ALU.subtract).then_inc(w_lo, 1)

                dve.sem_inc(y_done, 2)

                def piece(n, to_hi, to, j, q):
                    dve.wait_ge(piece_hi, n + 1)
                    v.tensor_tensor(to[:, j, 4 * q:4 * q + 4, :], ps_t[q][:].rearrange("p (k n) -> p k n", k=4),
                                    to_hi[:, j, 4 * q:4 * q + 4, :].bitcast(F32), ALU.subtract).then_inc(piece_lo, 1)

                def pieces2(n, to_hi, to, second, q):
                    with dve.If(second == 1):
                        piece(n, to_hi, to, 1, q)
                    with dve.Else():
                        dve.wait_ge(piece_lo, n)
                        dve.sem_inc(piece_lo, 1)

                def rows_of(bias, c, nb):
                    return bias[:, c * 512:c * 512 + 512].unsqueeze(1).to_broadcast([P, nb, 512])

                def take_glu(s, c, bank, nb, done, units):
                    g = glu[:, 0:nb, c * 512:c * 512 + 512]
                    dve.wait_ge(half_done, done)
                    if not isinstance(s, int):
                        dve.wait_ge(hid_done, 2 * s)
                    dve.wait_ge(up_bias_loaded, 32 * (s + 1))
                    v.tensor_tensor(g, ps_u[bank][:, 0:nb], rows_of(bias_g, c, nb), ALU.add).then_inc(unit_taken, 1)
                    dve.wait_ge(unit_taken, units + 1)
                    v.tensor_scalar(g, g, LIMIT, None, ALU.min).then_inc(clipped, 1)

                def swish(s, c, nb):
                    g = glu[:, 0:nb, c * 512:c * 512 + 512]
                    dve.wait_ge(sig_done, 2 * s + c + 1)
                    v.tensor_tensor(g, g, sig[:, 0:nb], ALU.mult).then_inc(swished, 1)

                def take_lin(s, c, bank, nb, done, units):
                    dve.wait_ge(half_done, done)
                    if not isinstance(s, int) or c:
                        dve.wait_ge(hid_done, 2 * s + c)
                    v.tensor_tensor(lin[:, 0:nb], ps_u[bank][:, 0:nb], rows_of(bias_l, c, nb), ALU.add).then_inc(unit_taken, 1)
                    dve.wait_ge(unit_taken, units + 1)
                    v.tensor_scalar(lin[:, 0:nb], lin[:, 0:nb], LIMIT, -LIMIT, ALU.min, ALU.max).then_inc(lin_clipped, 1)
                    dve.wait_ge(lin_clipped, 2 * s + c + 1)
                    dve.wait_ge(swished, 2 * s + c + 1)
                    v.scalar_tensor_tensor(out=hid[:, 0:nb, c * 512:c * 512 + 512], in0=lin[:, 0:nb], scalar=1.0,
                                           in1=glu[:, 0:nb, c * 512:c * 512 + 512], op0=ALU.add, op1=ALU.mult).then_inc(hid_done, 1)

                def take_down(s, c, bank, nb, done):
                    dve.wait_ge(y_free, s + 1)
                    dve.wait_ge(half_done, done)
                    dve.wait_ge(down_bias_loaded, 16 * (s + 1))
                    v.tensor_tensor(y[:, 0:nb, c * 512:c * 512 + 512], ps_u[bank][:, 0:nb], rows_of(bias_d, c, nb), ALU.add).then_inc(y_done, 1)

                def turn(s, first):
                    base = 0 if first else halves_before(s)
                    units = 0 if first else units_before(s)
                    second, second_next = second_at(dve, s), second_at(dve, s + 1)
                    if not first:
                        second_last = second_at(dve, s - 1)
                    P0 = 4 if first else 8 * s

                    def bank(n):
                        return n % BANKS if first else unit_bank(n)

                    def evacuate(i):
                        if i in (2, 4):
                            for_blocks(dve, second, lambda nb: take_glu(s, i // 2 - 1, bank(i // 2 - 1), nb, base + i, 4 * s + i // 2 - 1))
                        if i in (4, 6):
                            for_blocks(dve, second, lambda nb: swish(s, i // 2 - 2, nb))
                        if i in (6, 8):
                            for_blocks(dve, second, lambda nb: take_lin(s, i // 2 - 3, bank(i // 2 - 1), nb, base + i, 4 * s + i // 2 - 1))
                        if i in (10, 12) and not first:
                            for_blocks(dve, second_last, lambda nb: take_down(s - 1, i // 2 - 5, bank(i // 2 - 1), nb, base + i))

                    for i in range(UP if first else TURN):
                        if not first:
                            if i in (2, 3):
                                piece(P0 + i - 2, hTh, hTl, 0, i - 2)
                            if i in (4, 5):
                                pieces2(P0 + i - 2, hTh, hTl, second_last, i - 4)
                            if i in (8, 9):
                                piece(P0 + i - 4, xTh, xTl, 0, i - 8)
                            if i in (10, 11):
                                pieces2(P0 + i - 4, xTh, xTl, second_next, i - 10)
                        evacuate(i)
                        split(i + LEAD, base)
                    if first:
                        for q in (0, 1):
                            piece(P0 + q, xTh, xTl, 0, q)
                        for q in (0, 1):
                            pieces2(P0 + 2 + q, xTh, xTl, second_next, q)
                    evacuate(UP if first else TURN)

                second = second_at(dve, 0)
                for q in (0, 1):
                    piece(q, xTh, xTl, 0, q)
                for q in (0, 1):
                    pieces2(2 + q, xTh, xTl, second, q)
                for h in range(LEAD):
                    split(h, 0)
                turn(0, True)
                with dve.Fori(1, count) as s:
                    turn(s, False)
                last = second_at(dve, count - 1)
                for q in (0, 1):
                    piece(8 * count + q, hTh, hTl, 0, q)
                for q in (0, 1):
                    pieces2(8 * count + 2 + q, hTh, hTl, last, q)
                split(LEAD, halves_before(count))
                for c in (0, 1):
                    for_blocks(dve, last, lambda nb: take_down(count - 1, c, unit_bank(c), nb, halves_before(count) + 2 * c + 2))

            @block.tensor
            def _(pe):
                count = groups_of(pe)

                def piece(n, of, j, q, guard=True):
                    if guard:
                        pe.wait_ge(piece_lo, n - 1)
                    for k in range(4):
                        c = (4 * q + k) * P
                        last = nc.tensor.transpose(ps_t[q][:, k * P:(k + 1) * P], of[:, j, c:c + P], ident[:])
                    last.then_inc(turned, 1)

                def pieces2(n, of, second, q):
                    with pe.If(second == 1):
                        piece(n, of, 1, q)
                    with pe.Else():
                        pe.wait_ge(turned, n)
                        pe.sem_inc(turned, 1)

                def half(stat_hi, stat_lo, slot, k_half, bank, nb):
                    for j in range(nb):
                        for kk in range(4):
                            k = 4 * k_half + kk
                            out = ps_u[bank][:, j]
                            nc.tensor.matmul(out, stat_hi[:, j, k, :], wh[:, slot, kk, :], start=(k == 0), stop=False)
                            nc.tensor.matmul(out, stat_hi[:, j, k, :], wl[:, slot, kk, :], start=False, stop=False)
                            last = nc.tensor.matmul(out, stat_lo[:, j, k, :], wh[:, slot, kk, :], start=False, stop=(k == KT - 1))
                    last.then_inc(half_done, 1)

                def turn(s, first):
                    base = 0 if first else halves_before(s)
                    second, second_next = second_at(pe, s), second_at(pe, s + 1)
                    if not first:
                        second_last = second_at(pe, s - 1)
                    P0 = 4 if first else 8 * s
                    for i in range(UP if first else TURN):
                        if not first:
                            if i == 2:
                                pe.wait_ge(hid_done, 2 * s)
                            if i in (2, 3):
                                piece(P0 + i - 2, hid, 0, i - 2)
                            if i in (4, 5):
                                pieces2(P0 + i - 2, hid, second_last, i - 4)
                            if i == 8:
                                for j in (0, 1):
                                    pe.wait_ge(rows_loaded[j], 16 * (s + 2))
                            if i in (8, 9):
                                piece(P0 + i - 4, rows, 0, i - 8)
                            if i in (10, 11):
                                pieces2(P0 + i - 4, rows, second_next, i - 10)
                        unit = i // 2
                        bank = unit % BANKS if first else unit_bank(unit)
                        if i % 2 == 0:
                            if unit >= 3:
                                pe.wait_ge(unit_taken, 4 * s + unit - 2)
                            elif not first:
                                if unit == 0:
                                    pe.wait_ge(unit_taken, 4 * s)
                                else:
                                    pe.wait_ge(y_done, 2 * s + unit - 2)
                        if i == 0:
                            pe.wait_ge(piece_lo, 4 if first else 8 * s)
                        if i == UP:
                            pe.wait_ge(piece_lo, P0 + 4)
                        pe.wait_ge(w_lo, base + i + 1)
                        operands = (xTh, xTl) if i < UP else (hTh, hTl)
                        for_blocks(pe, second if i < UP else second_last, lambda nb: half(*operands, i % SLOTS, i % 2, bank, nb))
                    if first:
                        for j in (0, 1):
                            pe.wait_ge(rows_loaded[j], 32)
                        for q in (0, 1):
                            piece(P0 + q, rows, 0, q)
                        for q in (0, 1):
                            pieces2(P0 + 2 + q, rows, second_next, q)

                second = second_at(pe, 0)
                for j in (0, 1):
                    pe.wait_ge(rows_loaded[j], 16)
                for q in (0, 1):
                    piece(q, rows, 0, q, guard=False)
                for q in (0, 1):
                    pieces2(2 + q, rows, second, q)
                turn(0, True)
                with pe.Fori(1, count) as s:
                    turn(s, False)
                last = second_at(pe, count - 1)
                pe.wait_ge(hid_done, 2 * count)
                for q in (0, 1):
                    piece(8 * count + q, hid, 0, q)
                for q in (0, 1):
                    pieces2(8 * count + 2 + q, hid, last, q)
                pe.wait_ge(piece_lo, 8 * count + 4)
                for i in range(TURN - UP):
                    if i == 0:
                        pe.wait_ge(unit_taken, 4 * count)
                    if i == 2:
                        pe.wait_ge(y_done, 2 * count - 1)
                    pe.wait_ge(w_lo, halves_before(count) + i + 1)
                    for_blocks(pe, last, lambda nb: half(hTh, hTl, i % SLOTS, i % 2, unit_bank(i // 2), nb))


def combine(nc, h_rows, y_rows, final_g, gate, out):
    with ExitStack() as ctx:
        def sb(name, shape, dt=F32):
            return ctx.enter_context(nc.sbuf_tensor(name, shape, dt))

        def sem(name):
            return ctx.enter_context(nc.semaphore(name))

        BUFS = 3
        ht, yt = sb("h_again", [P, BUFS, D]), sb("y_again", [P, BUFS, TOP_K, D])
        ot, gf = sb("out_tile", [P, 2, D]), sb("final_rows", [P, D])
        sq = sb("out_squares", [P, D])
        ss, rms, rstd, eps = sb("out_ss", [P, TILES]), sb("out_rms", [P, TILES]), sb("out_rstd", [P, TILES]), sb("eps3", [P, 1])
        h_loaded, y_loaded = [sem(f"h_again_loaded{i}") for i in range(BUFS)], [sem(f"y_again_loaded{i}") for i in range(BUFS)]
        g_loaded, eps_set, summed, squared, rooted, inverted = (sem(n) for n in ("final_loaded", "eps3_set", "y_summed", "out_squared", "out_rooted", "out_inverted"))
        normed, stored = sem("out_normed"), [sem(f"out_stored{i}") for i in range(2)]
        h_t, o_t = (a.rearrange("(t p) d -> t p d", p=P) for a in (h_rows, out))
        y_t = y_rows[0:SPARE].rearrange("(t p k) d -> t p k d", p=P, k=TOP_K)

        with nc.Block() as block:
            @block.sync
            def _(sp):
                sp.dma_start(gf[:], final_g.partition_broadcast(P)).then_inc(g_loaded, 16)
                for t in range(TILES + 1):
                    if t < TILES:
                        if t >= BUFS:
                            sp.wait_ge(normed, t - BUFS + 1)
                        sp.dma_start(yt[:, t % BUFS], y_t[t]).then_inc(y_loaded[t % BUFS], 16)
                        sp.dma_start(ht[:, t % BUFS], h_t[t]).then_inc(h_loaded[t % BUFS], 16)
                    if t:
                        sp.wait_ge(normed, t)
                        sp.dma_start(o_t[t - 1], ot[:, (t - 1) % 2]).then_inc(stored[(t - 1) % 2], 16)
                for i in (0, 1):
                    sp.wait_ge(stored[i], 16 * (TILES // 2))

            @block.vector
            def _(dve):
                nc.vector.memset(eps[:], EPS).then_inc(eps_set, 1)
                dve.wait_ge(g_loaded, 16)
                for t in range(TILES):
                    b = t % BUFS
                    dve.wait_ge(h_loaded[b], 16 * (t // BUFS + 1))
                    dve.wait_ge(y_loaded[b], 16 * (t // BUFS + 1))
                    for k in range(TOP_K):
                        if k:
                            dve.wait_ge(summed, TOP_K * t + k)
                        nc.vector.scalar_tensor_tensor(out=ht[:, b], in0=yt[:, b, k, :], scalar=gate[:, t, k:k + 1], in1=ht[:, b],
                                                       op0=ALU.mult, op1=ALU.add).then_inc(summed, 1)
                    dve.wait_ge(rooted, t + 1)
                    nc.vector.reciprocal(rstd[:, t:t + 1], rms[:, t:t + 1]).then_inc(inverted, 1)
                    dve.wait_ge(inverted, t + 1)
                    if t >= 2:
                        dve.wait_ge(stored[t % 2], 16 * (t // 2))
                    nc.vector.scalar_tensor_tensor(out=ot[:, t % 2], in0=ht[:, b], scalar=rstd[:, t:t + 1], in1=gf[:],
                                                   op0=ALU.mult, op1=ALU.mult).then_inc(normed, 1)

            @block.scalar
            def _(act):
                act.wait_ge(eps_set, 1)
                for t in range(TILES):
                    act.wait_ge(summed, TOP_K * (t + 1))
                    nc.scalar.activation(sq[:], ht[:, t % BUFS], ACT.Square, accum_out=ss[:, t:t + 1]).then_inc(squared, 1)
                    act.wait_ge(squared, t + 1)
                    nc.scalar.activation(rms[:, t:t + 1], ss[:, t:t + 1], ACT.Sqrt, bias=eps[:], scale=1.0 / D).then_inc(rooted, 1)


def make_ident(nc, ctx):
    ident = ctx.enter_context(nc.sbuf_tensor("ident", [P, P], F32))
    zeroed, done = (ctx.enter_context(nc.semaphore(n)) for n in ("ident_zeroed", "ident_done"))
    with nc.Block() as block:
        @block.gpsimd
        def _(pool):
            nc.gpsimd.memset(ident[:], 0.0).then_inc(zeroed, 1)
            pool.wait_ge(zeroed, 1)
            nc.gpsimd.affine_select(out=ident[:], in_=ident[:], compare_op=ALU.not_equal, fill=1.0, base=0,
                                    pattern=[[-1, P]], channel_multiplier=1).then_inc(done, 1)
            pool.wait_ge(done, 1)
    return ident


def build(nc, x, norm1_g, w_in, w_alpha_up, b_alpha, gla_norm_g, swa_sinks, swa_norm_g, w_out, norm2_g, w_router, b_router,
          w_glu, b_glu, w_lin, b_lin, w_down, b_down, final_g, out):
    h_rows, hn_rows, y_rows = (nc.dram_tensor(n, [r, D], F32).ap() for n, r in (("h_rows", SEQ), ("hn_rows", SEQ), ("y_rows", SPARE + GROUP_ROWS)))
    with ExitStack() as whole:
        def keep(name, shape, dt=F32):
            return whole.enter_context(nc.sbuf_tensor(name, shape, dt))

        ident = make_ident(nc, whole)
        logits, gate = keep("logits", [P, TILES, EXPERTS]), keep("gate", [P, TILES, TOP_K])
        token_of, pair_of = keep("token_of", [P, BLOCKS], U32), keep("pair_of", [P, BLOCKS], U32)
        group_expert, group_second, last_group = keep("group_expert", [1, GROUPS], I32), keep("group_second", [1, GROUPS], I32), keep("last_group", [1, 1], I32)
        with ExitStack() as mixer:
            def sb(name, shape, dt=F32):
                return mixer.enter_context(nc.sbuf_tensor(name, shape, dt))

            ra = sb("ra", [P, TILES, 512])
            with ExitStack() as attention:
                def at(name, shape):
                    return attention.enter_context(nc.sbuf_tensor(name, shape, F32, side="right"))

                qaT, kaT, va = at("qaT", [P, PAIRS, SEQ]), at("kaT", [P, PAIRS, SEQ]), at("va", [P, TILES, 512])
                qbT, kbT, vbz = at("qbT", [P, 4, SEQ]), at("kbT", [P, 1, SEQ]), at("vbz", [P, TILES, VZ])
                project(nc, x[0], norm1_g[0], w_in[0], ident, qaT, kaT, va, ra, qbT, kbT, vbz)
                cat = sb("cat", [P, TILES, D])
                gla(nc, w_alpha_up[0], b_alpha[0], ident, qaT, kaT, va, vbz, cat)
                swa(nc, swa_sinks[0], ident, qbT, kbT, vbz, cat)
            mix_out(nc, x[0], w_out[0], gla_norm_g[0], swa_norm_g[0], norm2_g[0], w_router[0], b_router[0], ident, ra, cat, logits, h_rows, hn_rows)
        dispatch(nc, logits, gate, token_of, pair_of, group_expert, group_second, last_group)
        experts(nc, hn_rows, w_glu[0], b_glu[0], w_lin[0], b_lin[0], w_down[0], b_down[0], ident, token_of, group_expert, group_second,
                last_group, pair_of, y_rows)
        combine(nc, h_rows, y_rows, final_g, gate, out[0])


_INS = ["x", "norm1_g", "w_in", "w_alpha_up", "b_alpha", "gla_norm_g", "swa_sinks", "swa_norm_g", "w_out", "norm2_g", "w_router",
        "b_router", "w_glu", "b_glu", "w_lin", "b_lin", "w_down", "b_down", "final_g"]


def kernel(**inputs):
    import numpy as np
    import concourse.bacc as bacc
    from concourse.bass_utils import run_bass_kernel_spmd

    nc = bacc.Bacc("TRN2", target_bir_lowering=False, num_devices=1)
    arrays, args = {}, []
    for name in _INS:
        a = np.ascontiguousarray(inputs[name])
        arrays[f"in_{name}"] = a
        args.append(nc.dram_tensor(f"in_{name}", a.shape, mybir.dt.from_np(a.dtype), kind="ExternalInput").ap())
    out = nc.dram_tensor("out", (1, SEQ, D), F32, kind="ExternalOutput").ap()
    build(nc, *args, out)
    r = run_bass_kernel_spmd(nc, [arrays], core_ids=[0])
    return r.results[0]["out"]
```

```python
from contextlib import ExitStack

import concourse.bass as bass
from concourse import mybir

F32, F32R = mybir.dt.float32, mybir.dt.float32r
I32, U32 = mybir.dt.int32, mybir.dt.uint32
ALU, ACT = mybir.AluOpType, mybir.ActivationFunctionType
AX_X = mybir.AxisListType.X

P = 128
SEQ, D = 1024, 1024
TILES = SEQ // P
KT = D // P
EPS = 1e-5

GLA_HEADS, GLA_DK, GLA_DV, RANK, CHUNK, TAU = 4, 64, 128, 16, 64, 16.0
PAIRS = GLA_HEADS // 2
CHUNKS = SEQ // CHUNK
SWA_HEADS, KV_HEADS, DH, WINDOW = 8, 2, 64, 128
GROUP = SWA_HEADS // KV_HEADS

QA, KA = 0, GLA_HEADS * GLA_DK
VA = 2 * KA
RA = VA + GLA_HEADS * GLA_DV
ZA = RA + GLA_HEADS * GLA_DV
QB = ZA + RANK
KB = QB + SWA_HEADS * DH
VB = KB + KV_HEADS * DH
VZ = KV_HEADS * DH + RANK

EXPERTS, TOP_K, DFF, LIMIT, ALPHA = 32, 4, 1024, 7.0, 1.702
SMALL = P // 2
GROUP_ROWS = 2 * P
MAX_GROUPS = (TOP_K * SEQ + EXPERTS * (GROUP_ROWS - 1)) // GROUP_ROWS
GROUPS = MAX_GROUPS + 1
BLOCKS = 2 * GROUPS
RAW = 6
SPARE = TOP_K * SEQ


def project(nc, x, norm1_g, w_in, ident, qaT, kaT, va, ra, qbT, kbT, vbz):
    HALF = KT // 2
    SLOTS = 4
    units = [
        ([(QA, 256)], True), ([(KA, 256)], True), ([(VB, 128), (ZA, RANK)], False),
        ([(VA, 256)], False), ([(VA + 256, 256)], False),
        ([(QB + DH * h, DH) for h in (0, 4, 1, 5)], True), ([(QB + DH * h, DH) for h in (2, 6, 3, 7)], True),
        ([(KB, 128)], True),
        ([(RA, 256)], False), ([(RA + 256, 256)], False),
    ]
    with ExitStack() as ctx:
        def sb(name, shape, dt=F32):
            return ctx.enter_context(nc.sbuf_tensor(name, shape, dt))

        def sem(name):
            return ctx.enter_context(nc.semaphore(name))

        uTh, uTl = sb("uTh", [P, KT, SEQ], F32R), sb("uTl", [P, KT, SEQ], F32R)
        raw = sb("w_in_raw", [P, SLOTS, HALF, 256])
        wh, wl = sb("w_in_hi", [P, SLOTS, HALF, 256], F32R), sb("w_in_lo", [P, SLOTS, HALF, 256], F32R)
        XB = 4
        xt = va[:].rearrange("p t n -> p (t n)").rearrange("p (b d) -> p b d", d=D)
        squares, xn = sb("x_squares", [P, D]), sb("x_normed", [P, 2, D])
        g1 = sb("norm1_rows", [P, D])
        ss, rms, rstd = sb("x_ss", [P, TILES]), sb("x_rms", [P, TILES]), sb("x_rstd", [P, TILES])
        eps = sb("eps1", [P, 1])
        pT = [ctx.enter_context(nc.psum_tensor(f"uT_ps{i}", [P, 512], F32)) for i in range(2)]
        OB = 6
        pO = [ctx.enter_context(nc.psum_tensor(f"proj_ps{i}", [P, 512], F32)) for i in range(OB)]
        turn_banks = (pT, pO[4:6])

        x_loaded = [sem(f"x_loaded{i}") for i in range(XB)]
        g1_loaded, eps_set, w_loaded = sem("g1_loaded"), sem("eps1_set"), [sem(f"w_in_loaded{i}") for i in range(SLOTS)]
        summed, rooted, inverted, normed = sem("x_summed"), sem("x_rooted"), sem("x_inverted"), sem("x_normed_s")
        uT_turned, uT_hi, uT_lo = sem("uT_turned"), sem("uT_hi"), sem("uT_lo")
        w_hi, w_lo, unit_done = sem("w_in_hi_s"), sem("w_in_lo_s"), sem("unit_done")
        out_done, act_out, dve_out = sem("proj_out_done"), sem("proj_act_out"), sem("proj_dve_out")

        w_rows = w_in.rearrange("(k p) n -> p k n", p=P)
        x_rows = x.rearrange("(t p) d -> t p d", p=P)

        outs = []
        for u, (cols, turned) in enumerate(units):
            if turned:
                for half in range(2):
                    for c in range(1 if u == 7 else 2):
                        dst = {0: qaT, 1: kaT, 5: qbT, 6: qbT, 7: kbT}[u]
                        row = c + (2 if u == 6 else 0)
                        outs.append((u, c, half, dst[:, row, half * 512:half * 512 + 512], 512))
            else:
                for t in range(TILES):
                    dst = {2: vbz[:, t, :], 3: va[:, t, 0:256], 4: va[:, t, 256:512], 8: ra[:, t, 0:256], 9: ra[:, t, 256:512]}[u]
                    outs.append((u, None, t, dst, VZ if u == 2 else 256))
        first_out = [min(n for n, o in enumerate(outs) if o[0] == u) for u in range(len(units))] + [len(outs)]

        with nc.Block() as block:
            @block.sync
            def _(sp):
                def load(h):
                    at = 0
                    for c0, n in units[h // 2][0]:
                        sp.dma_start(raw[:, h % SLOTS, :, at:at + n],
                                     w_rows[:, h % 2 * HALF:(h % 2 + 1) * HALF, c0:c0 + n]).then_inc(w_loaded[h % SLOTS], 16)
                        at += n

                for t in range(TILES):
                    if t >= XB:
                        sp.wait_ge(normed, t - XB + 1)
                        sp.wait_ge(summed, t - XB + 1)
                    sp.dma_start(xt[:, t % XB, :], x_rows[t]).then_inc(x_loaded[t % XB], 16)
                    if t == 0:
                        sp.dma_start(g1[:], norm1_g.partition_broadcast(P)).then_inc(g1_loaded, 16)
                    if t == XB - 1:
                        load(0)
                        load(1)
                for h in range(2, 2 * len(units)):
                    if h >= SLOTS:
                        sp.wait_ge(w_lo, h - SLOTS + 1)
                    load(h)



            def arrived(h):
                return 16 * sum(len(units[g // 2][0]) for g in range(h % SLOTS, h + 1, SLOTS))

            def width(u):
                return sum(n for _, n in units[u][0])

            @block.scalar
            def _(act):
                act.wait_ge(eps_set, 1)

                def stat(t):
                    act.wait_ge(x_loaded[t % XB], 16 * (t // XB + 1))
                    nc.scalar.activation(squares[:], xt[:, t % XB, :], ACT.Square, accum_out=ss[:, t:t + 1]).then_inc(summed, 1)
                    act.wait_ge(summed, t + 1)
                    nc.scalar.activation(rms[:, t:t + 1], ss[:, t:t + 1], ACT.Sqrt, bias=eps[:], scale=1.0 / D).then_inc(rooted, 1)

                def split(h):
                    act.wait_ge(w_loaded[h % SLOTS], arrived(h))
                    if h >= SLOTS:
                        act.wait_ge(unit_done, (h - SLOTS) // 2 + 1)
                    n = width(h // 2)
                    nc.scalar.activation(wh[:, h % SLOTS, :, 0:n], raw[:, h % SLOTS, :, 0:n], ACT.Copy).then_inc(w_hi, 1)

                stat(0)
                stat(1)
                for t in range(TILES):
                    if t == TILES // 2:
                        split(0)
                        split(1)
                    if t + 2 < TILES:
                        stat(t + 2)
                    for half in range(2):
                        act.wait_ge(uT_turned, 2 * t + half + 1)
                        nc.scalar.activation(uTh[:, half * 4:half * 4 + 4, t * P:(t + 1) * P],
                                             turn_banks[t % 2][half][:].rearrange("p (k n) -> p k n", k=4), ACT.Copy).then_inc(uT_hi, 1)

                for h in range(2, SLOTS):
                    split(h)
                for u in range(len(units)):
                    for n in range(first_out[u], first_out[u + 1]):
                        if n % 2 == 0:
                            act.wait_ge(out_done, n + 1)
                            nc.scalar.activation(outs[n][3], pO[n % OB][:, 0:outs[n][4]], ACT.Copy).then_inc(act_out, 1)
                    for h in (2 * u + SLOTS, 2 * u + SLOTS + 1):
                        if h < 2 * len(units):
                            split(h)

            @block.vector
            def _(dve):
                nc.vector.memset(eps[:], EPS).then_inc(eps_set, 1)
                dve.wait_ge(g1_loaded, 16)

                def norm(t):
                    dve.wait_ge(rooted, t + 1)
                    nc.vector.reciprocal(rstd[:, t:t + 1], rms[:, t:t + 1]).then_inc(inverted, 1)
                    dve.wait_ge(inverted, t + 1)
                    if t >= 2:
                        dve.wait_ge(uT_turned, 2 * (t - 1))
                    nc.vector.scalar_tensor_tensor(out=xn[:, t % 2, :], in0=xt[:, t % XB, :], scalar=rstd[:, t:t + 1], in1=g1[:],
                                                   op0=ALU.mult, op1=ALU.mult).then_inc(normed, 1)

                def split(h):
                    dve.wait_ge(w_hi, h + 1)
                    n = width(h // 2)
                    nc.vector.tensor_tensor(wl[:, h % SLOTS, :, 0:n], raw[:, h % SLOTS, :, 0:n],
                                            wh[:, h % SLOTS, :, 0:n].bitcast(F32), ALU.subtract).then_inc(w_lo, 1)

                norm(0)
                for t in range(TILES):
                    if t == TILES // 2:
                        split(0)
                        split(1)
                    if t + 1 < TILES:
                        norm(t + 1)
                    for half in range(2):
                        dve.wait_ge(uT_hi, 2 * t + half + 1)
                        nc.vector.tensor_tensor(uTl[:, half * 4:half * 4 + 4, t * P:(t + 1) * P],
                                                turn_banks[t % 2][half][:].rearrange("p (k n) -> p k n", k=4),
                                                uTh[:, half * 4:half * 4 + 4, t * P:(t + 1) * P].bitcast(F32),
                                                ALU.subtract).then_inc(uT_lo, 1)

                for h in range(2, SLOTS):
                    split(h)
                for u in range(len(units)):
                    for n in range(first_out[u], first_out[u + 1]):
                        if n % 2:
                            dve.wait_ge(out_done, n + 1)
                            nc.vector.tensor_copy(outs[n][3], pO[n % OB][:, 0:outs[n][4]]).then_inc(dve_out, 1)
                    for h in (2 * u + SLOTS, 2 * u + SLOTS + 1):
                        if h < 2 * len(units):
                            split(h)

            @block.tensor
            def _(pe):
                def turn(t):
                    pe.wait_ge(normed, t + 1)
                    for half in range(2):
                        if t >= 2:
                            pe.wait_ge(uT_lo, 2 * (t - 2) + half + 1)
                        for k in range(4):
                            c = (half * 4 + k) * P
                            last = nc.tensor.transpose(turn_banks[t % 2][half][:, k * P:(k + 1) * P], xn[:, t % 2, c:c + P], ident[:])
                        last.then_inc(uT_turned, 1)

                for t in range(TILES // 2):
                    turn(t)
                for n, (u, c, at, _, wide) in enumerate(outs):
                    if n == 0:
                        pe.wait_ge(uT_lo, TILES)
                    if n in (1, 2):
                        turn(TILES // 2 + 2 * (n - 1))
                        turn(TILES // 2 + 2 * (n - 1) + 1)
                    if n == 2:
                        pe.wait_ge(uT_lo, 2 * TILES)
                    if n == first_out[u]:
                        pe.wait_ge(w_lo, 2 * u + 2)
                    if n >= OB:
                        m = n - OB
                        pe.wait_ge(act_out if m % 2 == 0 else dve_out, m // 2 + 1)
                    acc = pO[n % OB][:, 0:wide]
                    for k in range(KT):
                        slot, kk = (2 * u + k // HALF) % SLOTS, k % HALF
                        if c is None:
                            rh, rl = (w[:, slot, kk, 0:wide] for w in (wh, wl))
                            sh, sl = (w[:, k, at * P:(at + 1) * P] for w in (uTh, uTl))
                        else:
                            rh, rl = (w[:, k, at * 512:at * 512 + 512] for w in (uTh, uTl))
                            sh, sl = (w[:, slot, kk, c * P:(c + 1) * P] for w in (wh, wl))
                        nc.tensor.matmul(acc, sh, rh, start=(k == 0), stop=False)
                        nc.tensor.matmul(acc, sh, rl, start=False, stop=False)
                        mm = nc.tensor.matmul(acc, sl, rh, start=False, stop=(k == KT - 1))
                    mm.then_inc(out_done, 1)
                    if n == first_out[u + 1] - 1:
                        pe.wait_ge(out_done, n + 1)
                        pe.sem_inc(unit_done, 1)


def gla(nc, w_alpha_up, b_alpha, ident, qaT, kaT, va, vbz, cat):
    with ExitStack() as ctx:
        def sb(name, shape, dt=F32):
            return ctx.enter_context(nc.sbuf_tensor(name, shape, dt))

        def sem(name):
            return ctx.enter_context(nc.semaphore(name))

        zT = sb("zT", [RANK, SEQ])
        w_up, b_up = sb("w_alpha", [RANK, PAIRS * P]), sb("b_alpha", [P, PAIRS])
        soft, gate, cum = (sb(n, [P, PAIRS, SEQ]) for n in ("softplus", "log_gate", "log_gate_sum"))
        grow, shrink = sb("exp_sum", [P, PAIRS, SEQ]), sb("exp_minus_sum", [P, PAIRS, SEQ])
        tail = soft
        kt = sb("k_tail", [P, TILES, PAIRS * P])
        restart = sb("chunk_restart", [P, SEQ])
        decay = sb("chunk_decay", [P, PAIRS, CHUNKS])
        states = [gate[:].rearrange("p a (c v) -> p (a c) v", v=GLA_DV), cum[:].rearrange("p a (c v) -> p (a c) v", v=GLA_DV)]
        causal = sb("causal", [P, GLA_HEADS, P], I32)
        ones = sb("ones_i", [P, GLA_HEADS, P], I32)
        att = sb("gla_scores", [P, 2, GLA_HEADS * P])
        ps = ctx.enter_context(nc.psum_tensor("gla_ps", [P, 8, 512], F32))

        def kv_bank(t, c):
            return (2 if t % 2 == 0 else 0) + c

        loaded, restart_set, causal_set, att_zeroed = sem("alpha_loaded"), sem("restart_set"), sem("causal_set"), sem("att_zeroed")
        z_turned, z_copied, pre_ready = sem("z_turned"), sem("z_copied"), sem("pre_ready")
        absed, softed, clipped, gated, summed, shifted = (sem(n) for n in ("abs_s", "soft_s", "clip_s", "gate_s", "sum_s", "shift_s"))
        grown, shrunk, tailed = sem("grow_s"), sem("shrink_s"), sem("tail_s")
        q_ready, kt_ready, k_ready, decay_ready = sem("q_ready"), sem("kt_ready"), sem("k_ready"), sem("decay_ready")
        kt_turned, kt_copied, kv_ready, state_ready = sem("kt_turned"), sem("kt_copied"), sem("kv_ready"), sem("state_ready")
        att_ready, att_masked, o_ready, o_copied = sem("att_ready"), sem("att_masked"), sem("o_ready"), sem("o_copied")

        with nc.Block() as block:
            @block.sync
            def _(sp):
                sp.dma_start(w_up[:], w_alpha_up).then_inc(loaded, 16)
                with nc.allow_non_contiguous_dma(reason="256 biases, one to a partition"):
                    sp.dma_start(b_up[:], b_alpha.rearrange("(c p) -> p c", p=P)).then_inc(loaded, 16)

            @block.gpsimd
            def _(pool):
                nc.gpsimd.memset(restart[:], 1.0).then_inc(restart_set, 1)
                pool.wait_ge(restart_set, 1)
                nc.gpsimd.memset(restart[:].rearrange("p (c n) -> p c n", n=CHUNK)[:, :, 0:1], 0.0).then_inc(restart_set, 1)
                nc.gpsimd.memset(ones[:], 1).then_inc(causal_set, 1)
                pool.wait_ge(causal_set, 1)
                nc.gpsimd.affine_select(out=causal[:], in_=ones[:], compare_op=ALU.is_ge, fill=0, base=0,
                                        pattern=[[0, GLA_HEADS], [1, P]], channel_multiplier=-1).then_inc(causal_set, 1)
                pool.wait_ge(causal_set, 2)
                nc.gpsimd.memset(causal[0:CHUNK, :, CHUNK:P], 0).then_inc(causal_set, 1)
                nc.gpsimd.memset(att[:], 0.0).then_inc(att_zeroed, 1)

            @block.scalar
            def _(act):
                act.wait_ge(loaded, 32)
                for c in range(PAIRS):
                    act.wait_ge(pre_ready, 2 * c + 2)
                    nc.scalar.activation(soft[:, c, :], ps[:, 2 + 2 * c:4 + 2 * c, :], ACT.Abs, bias=b_up[:, c:c + 1]).then_inc(absed, 1)
                for c in range(PAIRS):
                    act.wait_ge(absed, c + 1)
                    nc.scalar.activation(soft[:, c, :], soft[:, c, :], ACT.Exp, scale=-1.0).then_inc(softed, 1)
                for c in range(PAIRS):
                    act.wait_ge(softed, PAIRS)
                    nc.scalar.activation(soft[:, c, :], soft[:, c, :], ACT.Ln, bias=1.0).then_inc(softed, 1)
                for c in range(PAIRS):
                    act.wait_ge(summed, c + 1)
                    nc.scalar.activation(grow[:, c, :], cum[:, c, :], ACT.Exp, scale=1.0 / TAU).then_inc(grown, 1)
                    act.wait_ge(shifted, c + 1)
                    nc.scalar.activation(tail[:, c, :], tail[:, c, :], ACT.Exp, scale=1.0 / TAU).then_inc(tailed, 1)
                    nc.scalar.activation(shrink[:, c, :], cum[:, c, :], ACT.Exp, scale=-1.0 / TAU).then_inc(shrunk, 1)
                for n in range(4):
                    act.wait_ge(kt_turned, n + 1)
                    nc.scalar.activation(kt[:, 2 * n:2 * n + 2, :], ps[:, n % 2, :].rearrange("p (t c) -> p t c", t=2), ACT.Copy).then_inc(kt_copied, 1)
                for t in range(TILES):
                    act.wait_ge(o_ready, t + 1)
                    nc.scalar.activation(cat[:, t, 0:512].rearrange("p (a b v) -> p b a v", a=PAIRS, b=2),
                                         ps[:, 6:8, 0:256].rearrange("p b (a v) -> p b a v", a=PAIRS), ACT.Copy).then_inc(o_copied, 1)

            @block.vector
            def _(dve):
                dve.wait_ge(z_turned, 1)
                nc.vector.tensor_copy(zT[:], ps[0:RANK, 0:2, :].rearrange("p b n -> p (b n)")).then_inc(z_copied, 1)
                dve.wait_ge(loaded, 32)
                for c in range(PAIRS):
                    dve.wait_ge(absed, c + 1)
                    nc.vector.tensor_scalar(gate[:, c, :], ps[:, 2 + 2 * c:4 + 2 * c, :].rearrange("p b n -> p (b n)"), b_up[:, c:c + 1], 0.0,
                                            ALU.add, ALU.min).then_inc(clipped, 1)
                for c in range(PAIRS):
                    dve.wait_ge(softed, PAIRS + c + 1)
                    dve.wait_ge(clipped, c + 1)
                    nc.vector.tensor_tensor(gate[:, c, :], gate[:, c, :], soft[:, c, :], ALU.subtract).then_inc(gated, 1)
                    dve.wait_ge(gated, c + 1)
                    dve.wait_ge(restart_set, 2)
                    nc.vector.tensor_tensor_scan(cum[:, c, :], restart[:], gate[:, c, :], 0.0, ALU.mult, ALU.add).then_inc(summed, 1)
                    dve.wait_ge(summed, c + 1)
                    by_chunk = cum[:, c, :].rearrange("p (c n) -> p c n", n=CHUNK)
                    nc.vector.tensor_tensor(tail[:, c, :].rearrange("p (c n) -> p c n", n=CHUNK),
                                            by_chunk[:, :, CHUNK - 1:CHUNK].to_broadcast([P, CHUNKS, CHUNK]), by_chunk,
                                            ALU.subtract).then_inc(shifted, 1)
                for c in range(PAIRS):
                    dve.wait_ge(tailed, c + 1)
                    nc.vector.tensor_tensor(tail[:, c, :], kaT[:, c, :], tail[:, c, :], ALU.mult).then_inc(kt_ready, 1)
                    dve.wait_ge(kt_ready, c + 1)
                    dve.wait_ge(shrunk, c + 1)
                    nc.vector.tensor_tensor(kaT[:, c, :], kaT[:, c, :], shrink[:, c, :], ALU.mult).then_inc(k_ready, 1)
                    dve.wait_ge(grown, c + 1)
                    nc.vector.scalar_tensor_tensor(out=qaT[:, c, :], in0=qaT[:, c, :], scalar=GLA_DK ** -0.5, in1=grow[:, c, :],
                                                   op0=ALU.mult, op1=ALU.mult).then_inc(q_ready, 1)
                    nc.vector.tensor_copy(decay[:, c, :], grow[:, c, :].rearrange("p (c n) -> p c n", n=CHUNK)[:, :, CHUNK - 1]).then_inc(decay_ready, 1)
                dve.wait_ge(decay_ready, PAIRS)
                dve.wait_ge(att_zeroed, 1)
                dve.wait_ge(causal_set, 3)

                def mask(t):
                    dve.wait_ge(att_ready, t + 1)
                    if t >= 2:
                        dve.wait_ge(o_ready, t - 1)
                    nc.vector.copy_predicated(att[:, t % 2, :].rearrange("p (b n) -> p b n", b=2), causal[:].rearrange("p (b a) n -> p b (a n)", b=2),
                                              ps[:, 4:6, 0:256]).then_inc(att_masked, 1)

                for c in range(CHUNKS):
                    if c < CHUNKS - 1:
                        if c % 2 == 0:
                            dve.wait_ge(kv_ready, c // 2 + 1)
                        for pair in range(PAIRS):
                            kv = ps[:, kv_bank(c // 2, c % 2), pair * P:(pair + 1) * P]
                            if c == 0:
                                ins = nc.vector.tensor_copy(states[pair][:, c, :], kv)
                            else:
                                dve.wait_ge(state_ready, (c - 1) * PAIRS + pair + 1)
                                ins = nc.vector.scalar_tensor_tensor(out=states[pair][:, c, :], in0=states[pair][:, c - 1, :],
                                                                     scalar=decay[:, pair, c:c + 1], in1=kv, op0=ALU.mult, op1=ALU.add)
                            ins.then_inc(state_ready, 1)
                    if c % 2 == 0:
                        mask(c // 2)

            @block.tensor
            def _(pe):
                for t in range(TILES):
                    last = nc.tensor.transpose(ps[0:RANK, t // 4, (t % 4) * P:(t % 4 + 1) * P], vbz[:, t, P:VZ], ident[:])
                last.then_inc(z_turned, 1)
                pe.wait_ge(loaded, 32)
                pe.wait_ge(z_copied, 1)
                for c in range(PAIRS):
                    for half in range(2):
                        nc.tensor.matmul(ps[:, 2 + 2 * c + half, :], w_up[:, c * P:(c + 1) * P], zT[:, half * 512:half * 512 + 512],
                                         start=True, stop=True).then_inc(pre_ready, 1)
                pe.wait_ge(kt_ready, PAIRS)
                for n in range(4):
                    if n >= 2:
                        pe.wait_ge(kt_copied, n - 1)
                    for t in (0, 1):
                        for c in range(PAIRS):
                            last = nc.tensor.transpose(ps[:, n % 2, (t * PAIRS + c) * P:(t * PAIRS + c + 1) * P],
                                                       tail[:, c, (2 * n + t) * P:(2 * n + t + 1) * P], ident[:])
                    last.then_inc(kt_turned, 1)

                def kv(t):
                    if t >= 2:
                        pe.wait_ge(state_ready, 2 * PAIRS * (t - 1))
                    pe.wait_ge(kt_copied, 4)
                    for c in (0, 1):
                        for pair in range(PAIRS):
                            for h in (0, 1):
                                head = 2 * pair + h
                                last = nc.tensor.matmul(ps[h * 64:h * 64 + 64, kv_bank(t, c), pair * P:(pair + 1) * P],
                                                        kt[c * 64:c * 64 + 64, t, pair * P + h * 64:pair * P + h * 64 + 64],
                                                        va[c * 64:c * 64 + 64, t, head * P:(head + 1) * P], start=True, stop=True)
                    last.then_inc(kv_ready, 1)

                def scores(t):
                    if t:
                        pe.wait_ge(att_masked, t)
                    pe.wait_ge(q_ready, PAIRS)
                    pe.wait_ge(k_ready, PAIRS)
                    for head in range(GLA_HEADS):
                        part = slice(head % 2 * 64, head % 2 * 64 + 64)
                        last = nc.tensor.matmul(ps[:, 4 + head % 2, head // 2 * P:(head // 2 + 1) * P], kaT[part, head // 2, t * P:(t + 1) * P],
                                                qaT[part, head // 2, t * P:(t + 1) * P], start=True, stop=True)
                    last.then_inc(att_ready, 1)

                def mix(t):
                    pe.wait_ge(att_masked, t + 1)
                    if t:
                        pe.wait_ge(o_copied, t)
                    pe.wait_ge(state_ready, min(2 * t + 1, CHUNKS - 1) * PAIRS)
                    for head in range(GLA_HEADS):
                        part = slice(head % 2 * 64, head % 2 * 64 + 64)
                        out = ps[:, 6 + head % 2, head // 2 * P:(head // 2 + 1) * P]
                        at = (head % 2 * PAIRS + head // 2) * P
                        nc.tensor.matmul(out, att[:, t % 2, at:at + P], va[:, t, head * P:(head + 1) * P], start=True, stop=False,
                                         skip_group_check=True)
                        for c in (0, 1):
                            if 2 * t + c:
                                last = nc.tensor.matmul(out[c * 64:c * 64 + 64], qaT[part, head // 2, t * P + c * 64:t * P + c * 64 + 64],
                                                        states[head // 2][part, 2 * t + c - 1, :], start=False, stop=True,
                                                        skip_group_check=True)
                    last.then_inc(o_ready, 1)

                kv(0)
                scores(0)
                for t in range(TILES):
                    if t + 1 < TILES:
                        kv(t + 1)
                        scores(t + 1)
                    mix(t)


def swa(nc, swa_sinks, w_out, gla_norm_g, swa_norm_g, norm2_g, w_router, b_router, ident, qbT, kbT, vbz, cat, ra, wh, wl, gains, g2, w_r, b_r):
    units = [(n, g) for n in range(TILES) for g in range(KV_HEADS)]
    with ExitStack() as ctx:
        def sb(name, shape, dt=F32):
            return ctx.enter_context(nc.sbuf_tensor(name, shape, dt))

        def sem(name):
            return ctx.enter_context(nc.semaphore(name))

        rel = sb("distance", [P, 2 * WINDOW])
        bias = sb("alibi", [P, SWA_HEADS, 2 * WINDOW])
        sink = sb("sinks", [P, SWA_HEADS])
        s = sb("swa_scores", [P, 3, GROUP, 2 * WINDOW])
        pT = sb("swa_probs_T", [P, 2, 2, GROUP * P])
        top, low, es = sb("swa_max", [P, 3, GROUP]), sb("swa_minus_max", [P, 3, GROUP]), sb("sink_exp", [P, 3, GROUP])
        den = sb("swa_sum", [P, 3, GROUP])
        raw, sig = sb("w_out_raw", [P, 2, D]), sb("ra_sigmoid", [P, TILES, 512])
        ps_s = [ctx.enter_context(nc.psum_tensor(f"swa_s{i}", [P, GROUP, 2 * WINDOW], F32)) for i in range(2)]
        ps_t = [ctx.enter_context(nc.psum_tensor(f"swa_t{i}", [P, GROUP * P], F32)) for i in range(2)]
        ps_o = [ctx.enter_context(nc.psum_tensor(f"swa_o{i}", [P, 512], F32)) for i in range(2)]

        sinks_loaded, rel_done, sloped, bias_done = sem("sinks_loaded"), sem("rel_done"), sem("sloped"), sem("alibi_done")
        scored, biased, maxed, topped, lowed = (sem(n) for n in ("scored", "biased", "maxed", "topped", "lowed"))
        exped, sink_shifted, sink_exped, summed, inverted = (sem(n) for n in ("exped", "sink_shifted", "sink_exped", "swa_summed", "swa_inverted"))
        turned, copied0, copied1, mixed, scaled = (sem(n) for n in ("p_turned", "p_copied0", "p_copied1", "swa_mixed", "swa_scaled"))
        w_loaded, w_hi, w_lo = [sem(f"w_out_loaded{i}") for i in range(2)], sem("w_out_hi_s"), sem("w_out_lo_s")
        mix_loaded, sig_done = sem("gains_and_router_loaded"), sem("ra_sig_done")
        w_rows = w_out.rearrange("(k p) n -> k p n", p=P)

        def cols(n):
            return slice(0 if n else WINDOW, 2 * WINDOW)

        with nc.Block() as block:
            @block.sync
            def _(sp):
                sp.dma_start(sink[:], swa_sinks.partition_broadcast(P)).then_inc(sinks_loaded, 16)
                for h in range(GLA_HEADS):
                    sp.dma_start(gains[:, h * GLA_DV:(h + 1) * GLA_DV], gla_norm_g.partition_broadcast(P)).then_inc(mix_loaded, 16)
                for h in range(SWA_HEADS):
                    sp.dma_start(gains[:, 512 + h * DH:512 + (h + 1) * DH], swa_norm_g.partition_broadcast(P)).then_inc(mix_loaded, 16)
                sp.dma_start(g2[:], norm2_g.partition_broadcast(P)).then_inc(mix_loaded, 16)
                sp.dma_start(w_r[:], w_router.rearrange("(k p) e -> p k e", p=P)).then_inc(mix_loaded, 16)
                sp.dma_start(b_r[:], b_router.partition_broadcast(P)).then_inc(mix_loaded, 16)
                for k in range(KT):
                    if k >= 2:
                        sp.wait_ge(w_lo, k - 1)
                    sp.dma_start(raw[:, k % 2, :], w_rows[k]).then_inc(w_loaded[k % 2], 16)
                sp.wait_ge(mix_loaded, 16 * (GLA_HEADS + SWA_HEADS + 3))

            @block.gpsimd
            def _(pool):
                nc.gpsimd.iota(rel[:], pattern=[[-1, 2 * WINDOW]], base=WINDOW, channel_multiplier=1,
                               allow_small_or_imprecise_dtypes=True).then_inc(rel_done, 1)
                for h in range(SWA_HEADS):
                    pool.wait_ge(sloped, h + 1)
                    nc.gpsimd.affine_select(out=bias[:, h, :], in_=bias[:, h, :], compare_op=ALU.is_ge, fill=-3e38, base=WINDOW,
                                            pattern=[[-1, 2 * WINDOW]], channel_multiplier=1).then_inc(bias_done, 1)
                    pool.wait_ge(bias_done, 2 * h + 1)
                    nc.gpsimd.affine_select(out=bias[:, h, :], in_=bias[:, h, :], compare_op=ALU.is_gt, fill=-3e38, base=0,
                                            pattern=[[1, 2 * WINDOW]], channel_multiplier=-1).then_inc(bias_done, 1)
                for t in range(TILES):
                    pool.wait_ge(sig_done, t + 1)
                    nc.gpsimd.tensor_tensor(ra[:, t, :], ra[:, t, :], sig[:, t, :], ALU.mult)
                for k in range(KT):
                    pool.wait_ge(w_hi, k + 1)
                    nc.gpsimd.tensor_tensor(wl[:, k, :], raw[:, k % 2, :], wh[:, k, :].bitcast(F32), ALU.subtract).then_inc(w_lo, 1)

            @block.tensor
            def _(pe):
                def scores(u):
                    n, g = units[u]
                    if u >= 2:
                        pe.wait_ge(biased, u - 1)
                    part = slice(g * DH, (g + 1) * DH)
                    k0 = max(n - 1, 0) * P
                    for h in range(GROUP):
                        last = nc.tensor.matmul(ps_s[u % 2][:, h, cols(n)], qbT[part, h, n * P:(n + 1) * P], kbT[part, 0, k0:(n + 1) * P],
                                                start=True, stop=True)
                    last.then_inc(scored, 1)

                def turn(u):
                    n, g = units[u]
                    pe.wait_ge(exped, GROUP * (u + 1))
                    for half in (0, 1):
                        if u:
                            pe.wait_ge(copied1 if half else copied0, u)
                        for h in range(GROUP):
                            if half or n:
                                last = nc.tensor.transpose(ps_t[half][:, h * P:(h + 1) * P], s[:, u % 3, h, half * P:(half + 1) * P], ident[:])
                        if half or n:
                            last.then_inc(turned, 1)
                        else:
                            pe.sem_inc(turned, 1)

                def mix(u):
                    n, g = units[u]
                    pe.wait_ge(copied0, u + 1)
                    pe.wait_ge(copied1, u + 1)
                    if u >= 2:
                        pe.wait_ge(scaled, u - 1)
                    for h in range(GROUP):
                        out = ps_o[u % 2][:, h * DH:(h + 1) * DH]
                        if n:
                            nc.tensor.matmul(out, pT[:, u % 2, 0, h * P:(h + 1) * P], vbz[:, n - 1, g * DH:(g + 1) * DH], start=True, stop=False)
                        last = nc.tensor.matmul(out, pT[:, u % 2, 1, h * P:(h + 1) * P], vbz[:, n, g * DH:(g + 1) * DH], start=(n == 0), stop=True)
                    last.then_inc(mixed, 1)

                scores(0)
                scores(1)
                for u in range(len(units)):
                    if u + 2 < len(units):
                        scores(u + 2)
                    if u:
                        mix(u - 1)
                    turn(u)
                mix(len(units) - 1)

            @block.vector
            def _(dve):
                for h in range(SWA_HEADS):
                    dve.wait_ge(rel_done, 1)
                    nc.vector.tensor_scalar(bias[:, h, :], rel[:], -(2.0 ** (-8.0 * (h + 1) / SWA_HEADS)), None, ALU.mult).then_inc(sloped, 1)

                def scores(u):
                    n, g = units[u]
                    c, heads = cols(n), slice(g * GROUP, (g + 1) * GROUP)
                    dve.wait_ge(scored, u + 1)
                    if u >= 3:
                        dve.wait_ge(turned, 2 * (u - 2))
                    nc.vector.scalar_tensor_tensor(out=s[:, u % 3, :, c], in0=ps_s[u % 2][:, :, c], scalar=DH ** -0.5, in1=bias[:, heads, c],
                                                   op0=ALU.mult, op1=ALU.add).then_inc(biased, 1)
                    dve.wait_ge(biased, u + 1)
                    nc.vector.tensor_reduce(top[:, u % 3, :], s[:, u % 3, :, c], AX_X, ALU.max).then_inc(maxed, 1)
                    dve.wait_ge(maxed, u + 1)
                    nc.vector.tensor_tensor(top[:, u % 3, :], top[:, u % 3, :], sink[:, heads], ALU.max).then_inc(topped, 1)
                    dve.wait_ge(topped, u + 1)
                    nc.vector.tensor_scalar(low[:, u % 3, :], top[:, u % 3, :], -1.0, None, ALU.mult).then_inc(lowed, 1)
                    nc.vector.tensor_tensor(es[:, u % 3, :], sink[:, heads], top[:, u % 3, :], ALU.subtract).then_inc(sink_shifted, 1)

                def copy(u):
                    dve.wait_ge(turned, 2 * u + 2)
                    if u >= 2:
                        dve.wait_ge(mixed, u - 1)
                    nc.vector.tensor_copy(pT[:, u % 2, 1, :], ps_t[1][:]).then_inc(copied1, 1)
                    dve.wait_ge(sink_exped, u + 1)
                    nc.vector.tensor_tensor(den[:, u % 3, :], den[:, u % 3, :], es[:, u % 3, :], ALU.add).then_inc(summed, 1)
                    dve.wait_ge(summed, u + 1)
                    nc.vector.reciprocal(den[:, u % 3, :], den[:, u % 3, :]).then_inc(inverted, 1)

                def scale(u):
                    n, g = units[u]
                    dve.wait_ge(inverted, u + 1)
                    dve.wait_ge(mixed, u + 1)
                    nc.vector.tensor_tensor(cat[:, n, 512 + g * 256:512 + g * 256 + 256].rearrange("p (h c) -> p h c", c=DH),
                                            ps_o[u % 2][:, 0:256].rearrange("p (h c) -> p h c", c=DH),
                                            den[:, u % 3, :].unsqueeze(2).to_broadcast([P, GROUP, DH]), ALU.mult).then_inc(scaled, 1)

                dve.wait_ge(sinks_loaded, 16)
                dve.wait_ge(bias_done, 2 * SWA_HEADS)
                scores(0)
                scores(1)
                for u in range(len(units)):
                    if u + 2 < len(units):
                        scores(u + 2)
                    if u:
                        scale(u - 1)
                    copy(u)
                scale(len(units) - 1)

            @block.scalar
            def _(act):
                def exps(u):
                    n, g = units[u]
                    c = cols(n)
                    act.wait_ge(lowed, u + 1)
                    if u >= 3:
                        act.wait_ge(scaled, u - 2)
                    for h in range(GROUP):
                        nc.scalar.activation(s[:, u % 3, h, c], s[:, u % 3, h, c], ACT.Exp, bias=low[:, u % 3, h:h + 1],
                                             accum_out=den[:, u % 3, h:h + 1]).then_inc(exped, 1)
                    act.wait_ge(sink_shifted, u + 1)
                    nc.scalar.activation(es[:, u % 3, :], es[:, u % 3, :], ACT.Exp).then_inc(sink_exped, 1)

                for t in range(TILES):
                    nc.scalar.activation(sig[:, t, :], ra[:, t, :], ACT.Sigmoid).then_inc(sig_done, 1)
                exps(0)
                for u in range(len(units)):
                    if u + 1 < len(units):
                        exps(u + 1)
                    act.wait_ge(turned, 2 * u + 1)
                    if u >= 2:
                        act.wait_ge(mixed, u - 1)
                    if units[u][0]:
                        nc.scalar.activation(pT[:, u % 2, 0, :], ps_t[0][:], ACT.Copy).then_inc(copied0, 1)
                    else:
                        act.sem_inc(copied0, 1)
                    if u % KV_HEADS == 1:
                        k = u // KV_HEADS
                        act.wait_ge(w_loaded[k % 2], 16 * (k // 2 + 1))
                        nc.scalar.activation(wh[:, k, :], raw[:, k % 2, :], ACT.Copy).then_inc(w_hi, 1)


def mix_out(nc, x, ident, ra, cat, wh, wl, gains, g2, w_r, b_r, logits, h_rows, hn_rows):
    GG = GLA_HEADS + SWA_HEADS
    with ExitStack() as ctx:
        def sb(name, shape, dt=F32):
            return ctx.enter_context(nc.sbuf_tensor(name, shape, dt))

        def sem(name):
            return ctx.enter_context(nc.semaphore(name))

        xt, ht = sb("x_again", [P, D]), sb("h_tile", [P, D])
        hn = sb("hn_tile", [P, D])
        cTh, cTl = sb("catT_hi", [P, 2, KT, P], F32R), sb("catT_lo", [P, 2, KT, P], F32R)
        hnT = sb("hnT", [P, KT, P])
        ss, rms, rstd = (sb(n, [P, GG]) for n in ("head_ss", "head_rms", "head_rstd"))
        ss2, rms2, rstd2 = (sb(n, [P, TILES]) for n in ("h_ss", "h_rms", "h_rstd"))
        eps, eps_g = sb("eps2", [P, 1]), sb("eps_gla", [P, 1])
        sq = sb("squares", [P, D])
        ps_t = [ctx.enter_context(nc.psum_tensor(f"out_t{i}", [P, 512], F32)) for i in range(2)]
        ps_h = [ctx.enter_context(nc.psum_tensor(f"out_h{i}", [P, D], F32)) for i in range(2)]
        ps_l = ctx.enter_context(nc.psum_tensor("out_logits", [P, 512], F32))

        x_loaded, eps_set = sem("x_again_loaded"), sem("eps2_set")
        squared, grouped, rooted, inverted = sem("squared"), sem("grouped"), sem("head_rooted"), sem("head_inverted")
        scaled, gained, gated = sem("head_scaled"), sem("head_gained"), sem("head_gated")
        turned, t_hi, t_lo = sem("cat_turned"), sem("catT_hi_s"), sem("catT_lo_s")
        h_ready, h_added, h_squared, h_rooted, h_inverted = sem("h_ready"), sem("h_added"), sem("h_squared"), sem("h_rooted"), sem("h_inverted")
        hn_done, hn_turned, hnT_done, logit_ready, logit_done = sem("hn_done"), sem("hn_turned"), sem("hnT_done"), sem("logit_ready"), sem("logit_done")
        h_stored, hn_stored = sem("h_stored"), sem("hn_stored")

        x_t, h_t, hn_t = (a.rearrange("(t p) d -> t p d", p=P) for a in (x, h_rows, hn_rows))

        with nc.Block() as block:
            @block.sync
            def _(sp):
                for t in range(TILES):
                    if t:
                        sp.wait_ge(h_added, 2 * t)
                    sp.dma_start(xt[:], x_t[t]).then_inc(x_loaded, 16)
                    sp.wait_ge(hn_done, t + 1)
                    sp.dma_start(h_t[t], ht[:]).then_inc(h_stored, 16)
                    sp.dma_start(hn_t[t], hn[:]).then_inc(hn_stored, 16)
                sp.wait_ge(h_stored, 16 * TILES)
                sp.wait_ge(hn_stored, 16 * TILES)

            @block.scalar
            def _(act):
                act.wait_ge(eps_set, 1)

                def root(t):
                    if t:
                        act.wait_ge(grouped, 2 * t)
                    nc.scalar.activation(sq[:], cat[:, t, :], ACT.Square).then_inc(squared, 1)
                    act.wait_ge(grouped, 2 * t + 2)
                    if t:
                        act.wait_ge(inverted, t)
                    nc.scalar.activation(rms[:, 0:GLA_HEADS], ss[:, 0:GLA_HEADS], ACT.Sqrt, bias=eps[:], scale=1.0 / GLA_DV).then_inc(rooted, 1)
                    nc.scalar.activation(rms[:, GLA_HEADS:GG], ss[:, GLA_HEADS:GG], ACT.Sqrt, bias=eps[:], scale=1.0 / DH).then_inc(rooted, 1)

                def turn(t):
                    for half in range(2):
                        act.wait_ge(turned, 2 * t + half + 1)
                        if t >= 2:
                            act.wait_ge(h_ready, t - 1)
                        nc.scalar.activation(cTh[:, t % 2, half * 4:half * 4 + 4, :], ps_t[half][:].rearrange("p (k n) -> p k n", k=4),
                                             ACT.Copy).then_inc(t_hi, 1)

                def hnT_out(t):
                    for half in range(2):
                        act.wait_ge(hn_turned, 2 * t + half + 1)
                        if t:
                            act.wait_ge(logit_ready, t)
                        nc.scalar.activation(hnT[:, half * 4:half * 4 + 4, :], ps_t[half][:].rearrange("p (k n) -> p k n", k=4),
                                             ACT.Copy).then_inc(hnT_done, 1)

                root(0)
                turn(0)
                root(1)
                for t in range(TILES):
                    if t + 1 < TILES:
                        turn(t + 1)
                    if t + 2 < TILES:
                        root(t + 2)
                    if t:
                        hnT_out(t - 1)
                    act.wait_ge(h_added, 2 * t + 2)
                    if t:
                        act.wait_ge(hn_stored, 16 * t)
                        act.wait_ge(hn_turned, 2 * t)
                    nc.scalar.activation(hn[:], ht[:], ACT.Square, accum_out=ss2[:, t:t + 1]).then_inc(h_squared, 1)
                    act.wait_ge(h_squared, t + 1)
                    nc.scalar.activation(rms2[:, t:t + 1], ss2[:, t:t + 1], ACT.Sqrt, bias=eps[:], scale=1.0 / D).then_inc(h_rooted, 1)
                hnT_out(TILES - 1)

            @block.vector
            def _(dve):
                nc.vector.memset(eps[:], EPS).then_inc(eps_set, 1)


                def norm(t):
                    dve.wait_ge(squared, t + 1)
                    if t:
                        dve.wait_ge(rooted, 2 * t)
                    nc.vector.reduce_sum(ss[:, 0:GLA_HEADS], sq[:, 0:512].rearrange("p (h v) -> p h v", v=GLA_DV), AX_X).then_inc(grouped, 1)
                    nc.vector.reduce_sum(ss[:, GLA_HEADS:GG], sq[:, 512:D].rearrange("p (h v) -> p h v", v=DH), AX_X).then_inc(grouped, 1)
                    dve.wait_ge(rooted, 2 * t + 2)
                    if t:
                        dve.wait_ge(scaled, 2 * t)
                    nc.vector.reciprocal(rstd[:], rms[:]).then_inc(inverted, 1)
                    dve.wait_ge(inverted, t + 1)
                    a = cat[:, t, 0:512].rearrange("p (h v) -> p h v", v=GLA_DV)
                    b = cat[:, t, 512:D].rearrange("p (h v) -> p h v", v=DH)
                    nc.vector.tensor_tensor(a, a, rstd[:, 0:GLA_HEADS].unsqueeze(2).to_broadcast([P, GLA_HEADS, GLA_DV]), ALU.mult).then_inc(scaled, 1)
                    nc.vector.tensor_tensor(b, b, rstd[:, GLA_HEADS:GG].unsqueeze(2).to_broadcast([P, SWA_HEADS, DH]), ALU.mult).then_inc(scaled, 1)
                    dve.wait_ge(scaled, 2 * t + 2)
                    nc.vector.tensor_tensor(cat[:, t, :], cat[:, t, :], gains[:], ALU.mult).then_inc(gained, 1)
                    dve.wait_ge(gained, t + 1)
                    nc.vector.tensor_tensor(cat[:, t, 0:512], cat[:, t, 0:512], ra[:, t, :], ALU.mult).then_inc(gated, 1)

                def turn(t):
                    for half in range(2):
                        dve.wait_ge(t_hi, 2 * t + half + 1)
                        nc.vector.tensor_tensor(cTl[:, t % 2, half * 4:half * 4 + 4, :], ps_t[half][:].rearrange("p (k n) -> p k n", k=4),
                                                cTh[:, t % 2, half * 4:half * 4 + 4, :].bitcast(F32), ALU.subtract).then_inc(t_lo, 1)

                def add_bias(t):
                    dve.wait_ge(logit_ready, t + 1)
                    nc.vector.tensor_tensor(logits[:, t, :], ps_l[:, 0:EXPERTS], b_r[:], ALU.add).then_inc(logit_done, 1)

                norm(0)
                turn(0)
                norm(1)
                for t in range(TILES):
                    if t + 1 < TILES:
                        turn(t + 1)
                    if t + 2 < TILES:
                        norm(t + 2)
                    dve.wait_ge(h_ready, t + 1)
                    dve.wait_ge(x_loaded, 16 * (t + 1))
                    if t:
                        dve.wait_ge(h_stored, 16 * t)
                    for half in range(2):
                        c = slice(half * 512, half * 512 + 512)
                        nc.vector.tensor_tensor(ht[:, c], ps_h[t % 2][:, c], xt[:, c], ALU.add).then_inc(h_added, 1)
                    dve.wait_ge(h_rooted, t + 1)
                    nc.vector.reciprocal(rstd2[:, t:t + 1], rms2[:, t:t + 1]).then_inc(h_inverted, 1)
                    dve.wait_ge(h_inverted, t + 1)
                    nc.vector.scalar_tensor_tensor(out=hn[:], in0=ht[:], scalar=rstd2[:, t:t + 1], in1=g2[:],
                                                   op0=ALU.mult, op1=ALU.mult).then_inc(hn_done, 1)
                    if t:
                        add_bias(t - 1)
                add_bias(TILES - 1)

            @block.tensor
            def _(pe):
                def turn(t):
                    pe.wait_ge(gated, t + 1)
                    for half in range(2):
                        if t in (1, 2):
                            pe.wait_ge(t_lo, 2 * (t - 1) + half + 1)
                        elif t:
                            pe.wait_ge(hnT_done, 2 * (t - 3) + half + 1)
                        for k in range(4):
                            c = (half * 4 + k) * P
                            last = nc.tensor.transpose(ps_t[half][:, k * P:(k + 1) * P], cat[:, t, c:c + P], ident[:])
                        last.then_inc(turned, 1)

                def turn_hn(t):
                    pe.wait_ge(hn_done, t + 1)
                    for half in range(2):
                        if t + 2 < TILES:
                            pe.wait_ge(t_lo, 2 * (t + 2) + half + 1)
                        else:
                            pe.wait_ge(hnT_done, 2 * (t - 1) + half + 1)
                        for k in range(4):
                            c = (half * 4 + k) * P
                            last = nc.tensor.transpose(ps_t[half][:, k * P:(k + 1) * P], hn[:, c:c + P], ident[:])
                        last.then_inc(hn_turned, 1)

                def route(t):
                    pe.wait_ge(hnT_done, 2 * t + 2)
                    if t:
                        pe.wait_ge(logit_done, t)
                    for k in range(KT):
                        mm = nc.tensor.matmul(ps_l[:, 0:EXPERTS], hnT[:, k, :], w_r[:, k, :], start=(k == 0), stop=(k == KT - 1))
                    mm.then_inc(logit_ready, 1)

                turn(0)
                for t in range(TILES):
                    pe.wait_ge(t_lo, 2 * t + 2)
                    if t >= 2:
                        pe.wait_ge(h_added, 2 * (t - 1))
                    for k in range(KT):
                        if k == 2 and t + 1 < TILES:
                            turn(t + 1)
                        if k == 6 and t:
                            turn_hn(t - 1)
                        for half in range(2):
                            c = slice(half * 512, half * 512 + 512)
                            out = ps_h[t % 2][:, c]
                            nc.tensor.matmul(out, cTh[:, t % 2, k, :], wh[:, k, c], start=(k == 0), stop=False)
                            nc.tensor.matmul(out, cTh[:, t % 2, k, :], wl[:, k, c], start=False, stop=False)
                            mm = nc.tensor.matmul(out, cTl[:, t % 2, k, :], wh[:, k, c], start=False, stop=(k == KT - 1))
                    mm.then_inc(h_ready, 1)
                    if t:
                        route(t - 1)
                turn_hn(TILES - 1)
                route(TILES - 1)


def dispatch(nc, logits, gate, token_of, pair_of, group_expert, group_second, last_group, first_sem, up_weights, w_raw, w_loaded, ident):
    E, T = EXPERTS, TILES
    with ExitStack() as ctx:
        def sb(name, shape, dt=F32):
            return ctx.enter_context(nc.sbuf_tensor(name, shape, dt))

        def sem(name):
            return ctx.enter_context(nc.semaphore(name))

        best, where, where_f = sb("best", [P, T, 8]), sb("where", [P, T, 8], U32), sb("where_f", [P, T, 8])
        shifted, total = sb("gate_shifted", [P, T, TOP_K]), sb("gate_total", [P, T])
        e_iota, row_iota, pair_iota = sb("e_iota", [P, T, E]), sb("row_iota", [P, P]), sb("pair_iota", [P, TOP_K, T])
        spare_iota = sb("spare_iota", [P, BLOCKS])
        empty, pair_i = sb("row_empty", [P, BLOCKS]), sb("pair_i", [P, BLOCKS], I32)
        g_iota = sb("g_iota", [P, E])
        hot, mask, place, tmp = sb("hot", [P, TOP_K, T, E]), sb("routed", [P, T, E]), sb("place", [P, T, E]), sb("place_k", [P, TOP_K, T, E])
        below, ones = sb("below", [P, P]), sb("all_ones", [P, P])
        before = sb("tiles_before", [P, T + 1, E])
        ints, halves = sb("count_i", [P, E], I32), sb("half_i", [P, E], I32)
        n_groups, ends, starts, with_second, with_large = (sb(n, [P, E]) for n in ("n_groups", "group_ends", "group_starts", "with_second", "with_large"))
        dest_f, dest_i, low_f, block_f = sb("dest_f", [P, TOP_K, T]), sb("dest_i", [P, TOP_K, T], I32), sb("low_f", [P, TOP_K, T]), sb("block_f", [P, TOP_K, T])
        low_i = sb("low_i", [P, TOP_K, T], I32)
        J, R = sb("row_hot", [P, 4, P]), sb("block_hot", [P, 4, BLOCKS])
        cmp1, cmp2, cmp3 = (sb(n, [P, E]) for n in ("cmp1", "cmp2", "cmp3"))
        columns = sb("group_columns", [P, 2])
        ps_p = ctx.enter_context(nc.psum_tensor("place_ps", [P, 512], F32))
        ps_c = ctx.enter_context(nc.psum_tensor("count_ps", [P, 512], F32))
        ps_tok = ctx.enter_context(nc.psum_tensor("token_ps", [P, 512], F32))
        ps_g = ctx.enter_context(nc.psum_tensor("group_ps", [P, 512], F32))

        step, made, made0 = sem("dve_step"), sem("consts_made"), sem("ones_made")
        masked, prefixed = sem("routed_s"), sem("prefixed")
        gates_in, gates_exp = sem("gates_in"), sem("gates_exp")
        row_hot_ready, block_hot_ready, hot_used, tokens_ready = sem("row_hot_ready"), sem("block_hot_ready"), sem("hot_used"), sem("tokens_ready")
        columns_ready, groups_turned, groups_ready, dest_ready = sem("columns_ready"), sem("groups_turned"), sem("groups_ready"), sem("dest_ready")

        with nc.Block() as block:
            @block.sync
            def _(sp):
                sp.wait_ge(groups_ready, 1)
                expert = sp.value_load(group_expert[0:1, 0:1], min_val=0, max_val=E - 1)
                for n in range(RAW):
                    sp.dma_start(w_raw[:, n], half_unit(up_weights[n // 4], expert, n // 2 % 2, n % 2)).then_inc(w_loaded[n], 16)

            @block.gpsimd
            def _(pool):
                pool.sem_clear(range(first_sem, step.num))
                nc.gpsimd.memset(ones[:], 1.0).then_inc(made0, 1)
                pool.wait_ge(made0, 1)
                nc.gpsimd.affine_select(out=below[:], in_=ones[:], compare_op=ALU.is_gt, fill=0.0, base=0,
                                        pattern=[[1, P]], channel_multiplier=-1).then_inc(made, 1)
                pairs_plus_1, spare_plus_1 = pair_iota[:], spare_iota[:]
                for ap, pattern, mult in ((e_iota[:], [[0, T], [1, E]], 0), (row_iota[:], [[1, P]], 0), (pairs_plus_1, [[1, TOP_K], [TOP_K * P, T]], TOP_K),
                                          (g_iota[:], [[0, E]], 1), (spare_plus_1, [[0, GROUPS], [P, 2]], 1)):
                    base = 1 if ap is pairs_plus_1 else SPARE + 1 if ap is spare_plus_1 else 0
                    nc.gpsimd.iota(ap, pattern=pattern, base=base, channel_multiplier=mult, allow_small_or_imprecise_dtypes=True).then_inc(made, 1)
                pool.wait_ge(made, 6)
                pool.wait_ge(dest_ready, 1)
                for n in range(TOP_K * T):
                    k, t = n // T, n % T
                    if n >= 4:
                        pool.wait_ge(hot_used, n - 3)
                    nc.gpsimd.tensor_scalar(R[:, n % 4, :], row_iota[:, 0:BLOCKS], block_f[:, k, t:t + 1], pair_iota[:, k, t:t + 1],
                                            ALU.is_equal, ALU.mult).then_inc(block_hot_ready, 1)

            @block.scalar
            def _(act):
                act.wait_ge(gates_in, 1)
                nc.scalar.activation(shifted[:], shifted[:], ACT.Exp).then_inc(gates_exp, 1)

            @block.vector
            def _(dve):
                count = [0]

                def then(ins):
                    count[0] += 1
                    ins.then_inc(step, 1)
                    dve.wait_ge(step, count[0])

                v = nc.vector
                for t in range(T):
                    v.max(best[:, t, :], logits[:, t, :]).then_inc(step, 1)
                count[0] += T
                dve.wait_ge(step, count[0])
                for t in range(T):
                    v.max_index(where[:, t, :], best[:, t, :], logits[:, t, :]).then_inc(step, 1)
                count[0] += T
                dve.wait_ge(step, count[0])
                v.tensor_tensor(shifted[:], best[:, :, 0:TOP_K], best[:, :, 0:1].to_broadcast([P, T, TOP_K]), ALU.subtract).then_inc(gates_in, 1)
                then(v.tensor_copy(where_f[:], where[:]))
                dve.wait_ge(made, 6)
                for k in range(TOP_K):
                    v.tensor_tensor(hot[:, k], e_iota[:], where_f[:, :, k:k + 1].to_broadcast([P, T, E]), ALU.is_equal).then_inc(step, 1)
                count[0] += TOP_K
                dve.wait_ge(step, count[0])
                then(v.tensor_tensor(mask[:], hot[:, 0], hot[:, 1], ALU.add))
                then(v.tensor_tensor(mask[:], mask[:], hot[:, 2], ALU.add))
                v.tensor_tensor(mask[:], mask[:], hot[:, 3], ALU.add).then_inc(masked, 1)
                dve.wait_ge(gates_exp, 1)
                then(v.reduce_sum(total[:], shifted[:], AX_X))
                then(v.reciprocal(total[:], total[:]))
                then(v.tensor_tensor(gate[:], shifted[:], total[:].unsqueeze(2).to_broadcast([P, T, TOP_K]), ALU.mult))
                dve.wait_ge(prefixed, 2)
                then(v.memset(before[:, 0, :], 0.0))
                for t in range(T):
                    then(v.tensor_tensor(before[:, t + 1, :], before[:, t, :], ps_c[:, t * E:(t + 1) * E], ALU.add))
                then(v.tensor_tensor(place[:], ps_p[:, 0:T * E].rearrange("p (t e) -> p t e", t=T), before[:, 0:T, :], ALU.add))
                then(v.tensor_scalar(ints[:], before[:, T, :], float(GROUP_ROWS - 1), None, ALU.add))
                then(v.tensor_scalar(ints[:], ints[:], 8, None, ALU.arith_shift_right))
                then(v.tensor_copy(n_groups[:], ints[:]))
                then(v.tensor_scalar(halves[:], before[:, T, :], float(P - 1), None, ALU.add))
                then(v.tensor_scalar(halves[:], halves[:], 8, None, ALU.arith_shift_right))
                then(v.tensor_copy(with_second[:], halves[:]))
                then(v.tensor_scalar(halves[:], before[:, T, :], float(GROUP_ROWS - 1 - P - SMALL), None, ALU.add))
                then(v.tensor_scalar(halves[:], halves[:], 8, None, ALU.arith_shift_right))
                then(v.tensor_copy(with_large[:], halves[:]))
                then(v.tensor_tensor_scan(ends[:], ones[:, 0:E], n_groups[:], 0.0, ALU.mult, ALU.add))
                then(v.tensor_tensor(starts[:], ends[:], n_groups[:], ALU.subtract))
                then(v.tensor_scalar(n_groups[:], starts[:], float(GROUP_ROWS), None, ALU.mult))
                then(v.tensor_tensor(place[:], place[:], n_groups[:].unsqueeze(1).to_broadcast([P, T, E]), ALU.add))
                for k in range(TOP_K):
                    v.tensor_tensor(tmp[:, k], hot[:, k], place[:], ALU.mult).then_inc(step, 1)
                count[0] += TOP_K
                dve.wait_ge(step, count[0])
                then(v.reduce_sum(dest_f[:].rearrange("p k t -> p (k t)"), tmp[:].rearrange("p k t e -> p (k t) e"), AX_X))
                then(v.tensor_copy(dest_i[:], dest_f[:]))
                then(v.tensor_scalar(low_i[:], dest_i[:], P - 1, None, ALU.bitwise_and))
                then(v.tensor_scalar(dest_i[:], dest_i[:], 7, None, ALU.arith_shift_right))
                then(v.tensor_copy(block_f[:], dest_i[:]))
                dve.sem_inc(dest_ready, 1)
                then(v.tensor_copy(low_f[:], low_i[:]))
                then(v.tensor_tensor(cmp1[:], g_iota[:], ends[:], ALU.is_ge))
                then(v.reduce_sum(columns[:, 0:1], cmp1[:], AX_X))
                then(v.tensor_tensor(cmp1[:], g_iota[:], starts[:], ALU.subtract))
                then(v.tensor_tensor(cmp2[:], cmp1[:], with_second[:], ALU.is_lt))
                then(v.tensor_tensor(cmp3[:], cmp1[:], with_large[:], ALU.is_lt))
                then(v.tensor_tensor(cmp2[:], cmp2[:], cmp3[:], ALU.add))
                then(v.tensor_scalar(cmp1[:], cmp1[:], 0.0, None, ALU.is_ge))
                then(v.tensor_tensor(cmp1[:], cmp1[:], cmp2[:], ALU.mult))
                then(v.reduce_sum(columns[:, 1:2], cmp1[:], AX_X))
                dve.sem_inc(columns_ready, 1)
                then(v.tensor_scalar(last_group[:], ends[0:1, E - 1:E], -1.0, None, ALU.add))
                dve.wait_ge(groups_turned, 2)
                then(v.tensor_scalar(group_expert[:], ps_g[0:1, 0:GROUPS], float(E - 1), None, ALU.min))
                dve.sem_inc(groups_ready, 1)
                then(v.tensor_copy(group_second[:], ps_g[0:1, P:P + GROUPS]))
                for n in range(TOP_K * T):
                    k, t = n // T, n % T
                    if n >= 4:
                        dve.wait_ge(hot_used, n - 3)
                    v.tensor_scalar(J[:, n % 4, :], row_iota[:], low_f[:, k, t:t + 1], None, ALU.is_equal).then_inc(row_hot_ready, 1)
                dve.wait_ge(tokens_ready, 1)
                then(v.tensor_scalar(empty[:], ps_tok[:, 0:BLOCKS], 0.0, None, ALU.is_equal))
                then(v.tensor_tensor(empty[:], empty[:], spare_iota[:], ALU.mult))
                then(v.tensor_tensor(empty[:], ps_tok[:, 0:BLOCKS], empty[:], ALU.add))
                then(v.tensor_scalar(pair_i[:], empty[:], -1.0, None, ALU.add))
                then(v.tensor_copy(pair_of[:], pair_i[:]))
                then(v.tensor_scalar(pair_i[:], empty[:], -1.0, float(TOP_K * SEQ - 1), ALU.add, ALU.min))
                then(v.tensor_scalar(pair_i[:], pair_i[:], 2, None, ALU.arith_shift_right))
                then(v.tensor_copy(token_of[:], pair_i[:]))

            @block.tensor
            def _(pe):
                pe.wait_ge(masked, 1)
                pe.wait_ge(made, 1)
                rows = mask[:].rearrange("p t e -> p (t e)")
                nc.tensor.matmul(ps_p[:, 0:T * E], below[:], rows, start=True, stop=True).then_inc(prefixed, 1)
                nc.tensor.matmul(ps_c[:, 0:T * E], ones[:], rows, start=True, stop=True).then_inc(prefixed, 1)
                pe.wait_ge(columns_ready, 1)
                for i in (0, 1):
                    nc.tensor.matmul(ps_g[0:1, i * P:(i + 1) * P], columns[:, i:i + 1], ident[:], start=True, stop=True).then_inc(groups_turned, 1)
                for n in range(TOP_K * T):
                    pe.wait_ge(row_hot_ready, n + 1)
                    pe.wait_ge(block_hot_ready, n + 1)
                    mm = nc.tensor.matmul(ps_tok[:, 0:BLOCKS], J[:, n % 4, :], R[:, n % 4, :], start=(n == 0), stop=(n == TOP_K * T - 1))
                    mm.then_inc(hot_used, 1)
                pe.wait_ge(hot_used, TOP_K * T)
                pe.sem_inc(tokens_ready, 1)


def half_unit(matrices, expert, column_half, k_half):
    return (matrices.rearrange("e (k p) n -> e p k n", p=P)[bass.ds(expert, 1), :, k_half * 4:k_half * 4 + 4, column_half * 512:column_half * 512 + 512]
            .rearrange("e p k n -> p (e k) n"))


def experts(nc, w_raw, w_loaded, hn_rows, w_glu, b_glu, w_lin, b_lin, w_down, b_down, ident, token_of, group_expert, group_second, last_group, pair_of, y_rows, unused):
    SLOTS = 4
    LEAD = SLOTS - 1
    UP, TURN = 8, 12
    POOL_HALVES = (4, 8)
    BANKS = 3
    with ExitStack() as ctx:
        def sb(name, shape, dt=F32):
            return ctx.enter_context(nc.sbuf_tensor(name, shape, dt))

        def sem(name):
            return ctx.enter_context(nc.semaphore(name))

        raw = w_raw
        wh, wl = sb("w_hi", [P, SLOTS, 4, 512], F32R), sb("w_lo", [P, SLOTS, 4, 512], F32R)
        rows = sb("group_rows", [P, 2, D])
        xTh, xTl = sb("xT_hi", [P, 2, KT, P], F32R), sb("xT_lo", [P, 2, KT, P], F32R)
        hTh, hTl = sb("hidT_hi", [P, 2, KT, P], F32R), sb("hidT_lo", [P, 2, KT, P], F32R)
        glu, sig, lin = sb("glu", [P, 2, DFF]), sb("glu_sigmoid", [P, 2, 512]), sb("lin", [P, 2, 512])
        hid = sb("hidden", [P, 2, DFF])
        y = sb("y", [P, 2, D])
        bias_g, bias_l, bias_d = sb("glu_bias", [P, DFF]), sb("lin_bias", [P, DFF]), sb("down_bias", [P, D])
        ps_t = [ctx.enter_context(nc.psum_tensor(f"piece_ps{i}", [P, 512], F32)) for i in range(2)]
        ps_u = [ctx.enter_context(nc.psum_tensor(f"unit_ps{i}", [P, 2, 512], F32)) for i in range(BANKS)]

        w_hi, w_lo, w_lo_pool, half_done = sem("w_hi_s"), sem("w_lo_s"), sem("w_lo_pool_s"), sem("half_done")
        up_spread, down_spread, zeroed = sem("up_bias_spread"), sem("down_bias_spread"), sem("stale_rows_zeroed")
        unit_taken = sem("unit_taken")
        rows_loaded = [sem(f"rows_loaded{i}") for i in range(2)]
        turned, piece_hi, piece_lo = sem("piece_turned"), sem("piece_hi"), sem("piece_lo")
        up_bias_loaded, down_bias_loaded = sem("up_bias_loaded"), sem("down_bias_loaded")
        clipped, sig_done, swished = sem("glu_clipped"), sem("glu_sig_done"), sem("glu_swished")
        lin_clipped, hid_done = sem("lin_clipped"), sem("hid_done")
        act_ended, pool_waited = sem("act_ended"), sem("pool_waited")
        y_done, y_stored = sem("y_done"), sem("y_stored")
        y_free = sem("y_free")

        mats = (w_glu, w_lin, w_down)

        def halves_before(s):
            return TURN * s - (TURN - UP)

        def in_turn(n, first):
            return n + TURN - UP if first else n

        def raw_slot(n, first):
            return (in_turn(n, first) + 2) % RAW

        def loads_to(n, s, first):
            return n // RAW + 1 if first else 2 * s - 1 + (n + 8) // RAW

        def by_pool(n, first):
            return in_turn(n, first) % TURN in POOL_HALVES

        def wait_lo(eng, n, s, first):
            m = in_turn(n, first)
            pool_done = m // TURN * 2 + sum(m % TURN >= h for h in POOL_HALVES)
            if by_pool(n, first):
                eng.wait_ge(w_lo_pool, pool_done if first else 2 * s + pool_done)
            else:
                eng.wait_ge(w_lo, m - pool_done + 1 - (4 if first else 0) if first else 10 * s - 4 + m - pool_done + 1)

        def unit_bank(n):
            return (n - 2) % BANKS

        def groups_of(eng):
            return eng.value_load(last_group[0:1, 0:1], min_val=TOP_K * SEQ // GROUP_ROWS - 1, max_val=MAX_GROUPS - 1) + 1

        def expert_at(eng, s):
            return eng.value_load(group_expert[0:1, bass.ds(s, 1)], min_val=0, max_val=EXPERTS - 1)

        def second_at(eng, s):
            return eng.value_load(group_second[0:1, bass.ds(s, 1)], min_val=0, max_val=2)

        def for_blocks(eng, second, emit):
            with eng.If(second == 0):
                emit(1)
            with eng.Else():
                emit(2)

        def for_kinds(eng, second, emit):
            with eng.If(second == 0):
                emit(1, False)
            with eng.Else():
                with eng.If(second == 1):
                    emit(2, True)
                with eng.Else():
                    emit(2, False)

        with nc.Block() as block:
            @block.sync
            def _(sp):
                count = groups_of(sp)

                def load(n, s, first, matrix, expert):
                    slot, column_half, k_half = raw_slot(n, first), n // 2 % 2, n % 2
                    if not first or n >= RAW:
                        wait_lo(sp, n - RAW, s, first)
                    sp.dma_start(raw[:, slot], half_unit(mats[matrix], expert, column_half, k_half)).then_inc(w_loaded[slot], 16)

                def load_up(s, first):
                    expert = expert_at(sp, s)
                    for n in range(RAW if first else 0, UP):
                        load(n, s, first, n // 4, expert)

                load_up(0, True)
                with sp.Fori(1, count) as s:
                    load_up(s, False)
                    expert = expert_at(sp, s - 1)
                    for n in range(UP, TURN):
                        load(n, s, False, 2, expert)
                expert = expert_at(sp, count - 1)
                for n in range(TURN - UP):
                    load(n, count, False, 2, expert)

            @block.gpsimd
            def _(pool):
                count = groups_of(pool)
                indices, index_ready = sb("row_tokens", [P, 2], U32), sem("index_ready")
                places, place_ready = sb("row_pairs", [P, 2], U32), sem("place_ready")

                def gather(s):
                    second = second_at(pool, s)
                    nc.gpsimd.tensor_copy(indices[:], token_of[:, bass.ds(s * 2, 2)]).then_inc(index_ready, 1)
                    pool.wait_ge(index_ready, s + 1)
                    pool.sem_inc(pool_waited, 1)
                    def fetch(j):
                        pool.indirect_dma_start(rows[:, j, :], None, hn_rows, bass.IndirectOffsetOnAxis(ap=indices[:, j:j + 1], axis=0)
                                                ).then_inc(rows_loaded[j], 16)
                    fetch(0)
                    with pool.If(second == 0):
                        pool.dma_start(rows[0:1, 1, :], hn_rows[0:1, :]).then_inc(rows_loaded[1], 16)
                    with pool.Else():
                        fetch(1)

                def store(s):
                    second = second_at(pool, s)
                    nc.gpsimd.tensor_copy(places[:], pair_of[:, bass.ds(s * 2, 2)]).then_inc(place_ready, 1)
                    pool.wait_ge(place_ready, s + 1)
                    pool.wait_ge(y_done, 4 * s + 8)
                    pool.sem_inc(pool_waited, 1)

                    def send(j):
                        pool.indirect_dma_start(y_rows, bass.IndirectOffsetOnAxis(ap=places[:, j:j + 1], axis=0), y[:, j, :], None
                                                ).then_inc(y_stored, 16)
                    send(0)
                    with pool.If(second == 0):
                        pool.dma_start(unused[0:1], y[0:1, 1, :]).then_inc(y_stored, 16)
                    with pool.Else():
                        send(1)

                def split(n, s, first):
                    base = 0 if first else halves_before(s)
                    pool.wait_ge(w_hi, base + n + 1)
                    if not first or n >= SLOTS:
                        pool.wait_ge(half_done, base + n - SLOTS + 1)
                    nc.gpsimd.tensor_tensor(wl[:, n % SLOTS], raw[:, raw_slot(n, first)], wh[:, n % SLOTS].bitcast(F32), ALU.subtract
                                            ).then_inc(w_lo_pool, 1)

                def spread_up(s):
                    pool.wait_ge(up_bias_loaded, 32 * (s + 1))
                    pool.sem_inc(pool_waited, 1)
                    nc.gpsimd.partition_broadcast(bias_g[:], bias_g[0:1, :]).then_inc(up_spread, 1)
                    nc.gpsimd.partition_broadcast(bias_l[:], bias_l[0:1, :]).then_inc(up_spread, 1)

                def spread_down(s):
                    pool.wait_ge(down_bias_loaded, 16 * (s + 1))
                    pool.sem_inc(pool_waited, 1)
                    nc.gpsimd.partition_broadcast(bias_d[:], bias_d[0:1, :]).then_inc(down_spread, 1)

                gather(0)
                split(POOL_HALVES[0] - TURN + UP, 0, True)
                spread_up(0)
                for t in (glu, lin, y):
                    nc.gpsimd.memset(t[:, 1, :], 0.0).then_inc(zeroed, 1)
                pool.wait_ge(zeroed, 3)
                for j in (0, 1):
                    pool.dma_start(unused[j:j + 1], y[0:1, 1, :]).then_inc(y_stored, 16)
                pool.wait_ge(turned, 4)
                gather(1)
                split(POOL_HALVES[1] - TURN + UP, 0, True)
                spread_up(1)
                with pool.Fori(1, count) as s:
                    pool.wait_ge(turned, 8 * s)
                    gather(s + 1)
                    split(POOL_HALVES[0], s, False)
                    pool.wait_ge(y_stored, 32 * s)
                    pool.sem_inc(y_free, 1)
                    split(POOL_HALVES[1], s, False)
                    spread_down(s - 1)
                    spread_up(s + 1)
                    store(s - 1)
                spread_down(count - 1)
                pool.wait_ge(y_stored, 32 * count)
                pool.sem_inc(y_free, 1)
                store(count - 1)
                pool.wait_ge(y_stored, 32 * (count + 1))

            @block.scalar
            def _(act):
                count = groups_of(act)

                def split(n, s, first):
                    act.wait_ge(w_loaded[raw_slot(n, first)], 16 * loads_to(n, s, first))
                    if not first:
                        act.wait_ge(half_done, halves_before(s) + n - SLOTS + 1)
                    elif n >= SLOTS:
                        act.wait_ge(half_done, n - SLOTS + 1)
                    nc.scalar.activation(wh[:, n % SLOTS], raw[:, raw_slot(n, first)], ACT.Copy).then_inc(w_hi, 1)

                def sigmoid(s, c, nb, turns):
                    act.wait_ge(clipped, 2 * s + c + 1)
                    if turns or c:
                        act.wait_ge(swished, 2 * s + c)
                    nc.scalar.activation(sig[:, 0:nb], glu[:, 0:nb, c * 512:c * 512 + 512], ACT.Sigmoid, scale=ALPHA).then_inc(sig_done, 1)

                def piece(n, to, j, q):
                    act.wait_ge(turned, n + 1)
                    nc.scalar.activation(to[:, j, 4 * q:4 * q + 4, :], ps_t[q][:].rearrange("p (k n) -> p k n", k=4), ACT.Copy).then_inc(piece_hi, 1)

                def pieces2(n, to, second, q):
                    with act.If(second == 0):
                        act.wait_ge(piece_hi, n)
                        act.sem_inc(piece_hi, 1)
                    with act.Else():
                        with act.If(second == 1):
                            act.wait_ge(turned, n + 1)
                            nc.scalar.activation(to[:, 1, 4 * q:4 * q + 4, 0:SMALL], ps_t[q][:].rearrange("p (k n) -> p k n", k=4)[:, :, 0:SMALL],
                                                 ACT.Copy).then_inc(piece_hi, 1)
                        with act.Else():
                            piece(n, to, 1, q)

                def load_up_bias(s):
                    expert = expert_at(act, s)
                    for to, of in ((bias_g, b_glu), (bias_l, b_lin)):
                        act.dma_start(to[0:1, :], of[bass.ds(expert, 1), :]).then_inc(up_bias_loaded, 16)

                def turn(s, first):
                    second, second_next = second_at(act, s), second_at(act, s + 1)
                    if not first:
                        second_last, last_expert = second_at(act, s - 1), expert_at(act, s - 1)
                    P0 = 4 if first else 8 * s
                    for i in range(UP if first else TURN):
                        if i == 1 and not first:
                            act.wait_ge(y_done, 4 * s)
                            act.dma_start(bias_d[0:1, :], b_down[bass.ds(last_expert, 1), :]).then_inc(down_bias_loaded, 16)
                        if i in (3, 5):
                            for_blocks(act, second, lambda nb: sigmoid(s, (i - 3) // 2, nb, not first))
                        if not first:
                            if i in (2, 3):
                                piece(P0 + i - 2, hTh, 0, i - 2)
                            if i in (4, 5):
                                pieces2(P0 + i - 2, hTh, second_last, i - 4)
                            if i in (8, 9):
                                piece(P0 + i - 4, xTh, 0, i - 8)
                            if i in (10, 11):
                                pieces2(P0 + i - 4, xTh, second_next, i - 10)
                        split(i + LEAD, s, first)
                        if i == 9:
                            act.wait_ge(hid_done, 2 * s + 2)
                            load_up_bias(s + 1)
                    if first:
                        for q in (0, 1):
                            piece(P0 + q, xTh, 0, q)
                        for q in (0, 1):
                            pieces2(P0 + 2 + q, xTh, second_next, q)
                        act.wait_ge(hid_done, 2)
                        load_up_bias(1)

                load_up_bias(0)
                second = second_at(act, 0)
                for n in range(LEAD):
                    split(n, 0, True)
                for q in (0, 1):
                    piece(q, xTh, 0, q)
                for q in (0, 1):
                    pieces2(2 + q, xTh, second, q)
                turn(0, True)
                with act.Fori(1, count) as s:
                    turn(s, False)
                last, expert = second_at(act, count - 1), expert_at(act, count - 1)
                act.wait_ge(y_done, 4 * count)
                act.dma_start(bias_d[0:1, :], b_down[bass.ds(expert, 1), :]).then_inc(down_bias_loaded, 16)
                for q in (0, 1):
                    piece(8 * count + q, hTh, 0, q)
                for q in (0, 1):
                    pieces2(8 * count + 2 + q, hTh, last, q)
                split(LEAD, count, False)
                act.wait_ge(up_bias_loaded, 32 * (count + 1))
                act.wait_ge(down_bias_loaded, 16 * count)
                act.sem_inc(act_ended, 1)

            @block.vector
            def _(dve):
                count = groups_of(dve)
                v = nc.vector

                def split(n, s, first):
                    if by_pool(n, first):
                        return
                    base = 0 if first else halves_before(s)
                    dve.wait_ge(w_hi, base + n + 1)
                    if not first or n >= SLOTS:
                        dve.wait_ge(half_done, base + n - SLOTS + 1)
                    v.tensor_tensor(wl[:, n % SLOTS], raw[:, raw_slot(n, first)], wh[:, n % SLOTS].bitcast(F32), ALU.subtract).then_inc(w_lo, 1)

                dve.sem_inc(y_done, 4)

                def piece(n, to_hi, to, j, q):
                    dve.wait_ge(piece_hi, n + 1)
                    v.tensor_tensor(to[:, j, 4 * q:4 * q + 4, :], ps_t[q][:].rearrange("p (k n) -> p k n", k=4),
                                    to_hi[:, j, 4 * q:4 * q + 4, :].bitcast(F32), ALU.subtract).then_inc(piece_lo, 1)

                def pieces2(n, to_hi, to, second, q):
                    with dve.If(second == 0):
                        dve.wait_ge(piece_lo, n)
                        dve.sem_inc(piece_lo, 1)
                    with dve.Else():
                        with dve.If(second == 1):
                            dve.wait_ge(piece_hi, n + 1)
                            v.tensor_tensor(to_hi[:, 1, 4 * q:4 * q + 4, SMALL:2 * SMALL], ps_t[q][:].rearrange("p (k n) -> p k n", k=4)[:, :, 0:SMALL],
                                            to_hi[:, 1, 4 * q:4 * q + 4, 0:SMALL].bitcast(F32), ALU.subtract).then_inc(piece_lo, 1)
                        with dve.Else():
                            piece(n, to_hi, to, 1, q)

                def take(to, c, bias, bank, nb, small, sem, before, cols=None):
                    columns = slice(c * 512, c * 512 + 512)
                    cols = columns if cols is None else cols
                    if small:
                        v.tensor_tensor(to[0:SMALL, 1, cols], ps_u[bank][0:SMALL, 1], bias[0:SMALL, columns], ALU.add).then_inc(sem, 1)
                        v.tensor_tensor(to[:, 0, cols], ps_u[bank][:, 0], bias[:, columns], ALU.add)
                        dve.wait_ge(sem, before + 1)
                        v.tensor_tensor(to[0:SMALL, 1, cols], ps_u[bank][SMALL:2 * SMALL, 1], to[0:SMALL, 1, cols], ALU.add).then_inc(sem, 1)
                    else:
                        v.tensor_tensor(to[:, 0:nb, cols], ps_u[bank][:, 0:nb], bias[:, columns].unsqueeze(1).to_broadcast([P, nb, 512]), ALU.add).then_inc(sem, 2)

                def take_glu(s, c, bank, nb, small, done, units):
                    g = glu[:, 0:nb, c * 512:c * 512 + 512]
                    dve.wait_ge(half_done, done)
                    if not isinstance(s, int):
                        dve.wait_ge(hid_done, 2 * s)
                    dve.wait_ge(up_spread, 2 * (s + 1))
                    take(glu, c, bias_g, bank, nb, small, unit_taken, 2 * units)
                    dve.wait_ge(unit_taken, 2 * (units + 1))
                    v.tensor_scalar(g, g, LIMIT, None, ALU.min).then_inc(clipped, 1)

                def swish(s, c, nb):
                    g = glu[:, 0:nb, c * 512:c * 512 + 512]
                    dve.wait_ge(sig_done, 2 * s + c + 1)
                    v.tensor_tensor(g, g, sig[:, 0:nb], ALU.mult).then_inc(swished, 1)

                def take_lin(s, c, bank, nb, small, done, units):
                    dve.wait_ge(half_done, done)
                    if not isinstance(s, int) or c:
                        dve.wait_ge(hid_done, 2 * s + c)
                    take(lin, c, bias_l, bank, nb, small, unit_taken, 2 * units, cols=slice(0, 512))
                    dve.wait_ge(unit_taken, 2 * (units + 1))
                    v.tensor_scalar(lin[:, 0:nb], lin[:, 0:nb], LIMIT, -LIMIT, ALU.min, ALU.max).then_inc(lin_clipped, 1)
                    dve.wait_ge(lin_clipped, 2 * s + c + 1)
                    dve.wait_ge(swished, 2 * s + c + 1)
                    v.scalar_tensor_tensor(out=hid[:, 0:nb, c * 512:c * 512 + 512], in0=lin[:, 0:nb], scalar=1.0,
                                           in1=glu[:, 0:nb, c * 512:c * 512 + 512], op0=ALU.add, op1=ALU.mult).then_inc(hid_done, 1)

                def take_down(s, c, bank, nb, small, done):
                    dve.wait_ge(y_free, s + 1)
                    dve.wait_ge(half_done, done)
                    dve.wait_ge(down_spread, s + 1)
                    take(y, c, bias_d, bank, nb, small, y_done, 4 * s + 4 + 2 * c)

                def turn(s, first):
                    base = 0 if first else halves_before(s)
                    second, second_next = second_at(dve, s), second_at(dve, s + 1)
                    if not first:
                        second_last = second_at(dve, s - 1)
                    P0 = 4 if first else 8 * s

                    def bank(n):
                        return n % BANKS if first else unit_bank(n)

                    def evacuate(i):
                        if i in (2, 4):
                            for_kinds(dve, second, lambda nb, small: take_glu(s, i // 2 - 1, bank(i // 2 - 1), nb, small, base + i, 4 * s + i // 2 - 1))
                        if i in (4, 6):
                            for_blocks(dve, second, lambda nb: swish(s, i // 2 - 2, nb))
                        if i in (6, 8):
                            for_kinds(dve, second, lambda nb, small: take_lin(s, i // 2 - 3, bank(i // 2 - 1), nb, small, base + i, 4 * s + i // 2 - 1))
                        if i in (10, 12) and not first:
                            for_kinds(dve, second_last, lambda nb, small: take_down(s - 1, i // 2 - 5, bank(i // 2 - 1), nb, small, base + i))

                    for i in range(UP if first else TURN):
                        if not first:
                            if i in (2, 3):
                                piece(P0 + i - 2, hTh, hTl, 0, i - 2)
                            if i in (4, 5):
                                pieces2(P0 + i - 2, hTh, hTl, second_last, i - 4)
                            if i in (8, 9):
                                piece(P0 + i - 4, xTh, xTl, 0, i - 8)
                            if i in (10, 11):
                                pieces2(P0 + i - 4, xTh, xTl, second_next, i - 10)
                        evacuate(i)
                        split(i + LEAD, s, first)
                    evacuate(UP if first else TURN)
                    if first:
                        for q in (0, 1):
                            piece(P0 + q, xTh, xTl, 0, q)
                        for q in (0, 1):
                            pieces2(P0 + 2 + q, xTh, xTl, second_next, q)

                second = second_at(dve, 0)
                for n in range(LEAD):
                    split(n, 0, True)
                for q in (0, 1):
                    piece(q, xTh, xTl, 0, q)
                for q in (0, 1):
                    pieces2(2 + q, xTh, xTl, second, q)
                dve.wait_ge(zeroed, 3)
                turn(0, True)
                with dve.Fori(1, count) as s:
                    turn(s, False)
                last = second_at(dve, count - 1)
                for q in (0, 1):
                    piece(8 * count + q, hTh, hTl, 0, q)
                for q in (0, 1):
                    pieces2(8 * count + 2 + q, hTh, hTl, last, q)
                split(LEAD, count, False)
                for c in (0, 1):
                    for_kinds(dve, last, lambda nb, small: take_down(count - 1, c, unit_bank(c), nb, small, halves_before(count) + 2 * c + 2))

            @block.tensor
            def _(pe):
                count = groups_of(pe)

                def piece(n, of, j, q, guard=True):
                    if guard:
                        pe.wait_ge(piece_lo, n - 1)
                    for k in range(4):
                        c = (4 * q + k) * P
                        last = nc.tensor.transpose(ps_t[q][:, k * P:(k + 1) * P], of[:, j, c:c + P], ident[:])
                    last.then_inc(turned, 1)

                def pieces2(n, of, second, q):
                    with pe.If(second == 0):
                        pe.wait_ge(turned, n)
                        pe.sem_inc(turned, 1)
                    with pe.Else():
                        piece(n, of, 1, q)

                def half(stat_hi, stat_lo, slot, k_half, bank, nb, small):
                    for j in range(nb):
                        for kk in range(4):
                            k = 4 * k_half + kk
                            out = ps_u[bank][:, j]
                            if j and small:
                                nc.tensor.matmul(out, stat_hi[:, j, k, :], wh[:, slot, kk, :], start=(k == 0), stop=False)
                                last = nc.tensor.matmul(out, stat_hi[:, j, k, :], wl[:, slot, kk, :], start=False, stop=(k == KT - 1))
                                continue
                            nc.tensor.matmul(out, stat_hi[:, j, k, :], wh[:, slot, kk, :], start=(k == 0), stop=False)
                            nc.tensor.matmul(out, stat_hi[:, j, k, :], wl[:, slot, kk, :], start=False, stop=False)
                            last = nc.tensor.matmul(out, stat_lo[:, j, k, :], wh[:, slot, kk, :], start=False, stop=(k == KT - 1))
                    last.then_inc(half_done, 1)

                def turn(s, first):
                    second, second_next = second_at(pe, s), second_at(pe, s + 1)
                    if not first:
                        second_last = second_at(pe, s - 1)
                    P0 = 4 if first else 8 * s
                    for i in range(UP if first else TURN):
                        if not first:
                            if i == 2:
                                pe.wait_ge(hid_done, 2 * s)
                            if i in (2, 3):
                                piece(P0 + i - 2, hid, 0, i - 2)
                            if i in (4, 5):
                                pieces2(P0 + i - 2, hid, second_last, i - 4)
                            if i == 8:
                                for j in (0, 1):
                                    pe.wait_ge(rows_loaded[j], 16 * (s + 2))
                            if i in (8, 9):
                                piece(P0 + i - 4, rows, 0, i - 8)
                            if i in (10, 11):
                                pieces2(P0 + i - 4, rows, second_next, i - 10)
                        unit = i // 2
                        bank = unit % BANKS if first else unit_bank(unit)
                        if i % 2 == 0:
                            if unit >= 3:
                                pe.wait_ge(unit_taken, 2 * (4 * s + unit - 2))
                            elif not first:
                                if unit == 0:
                                    pe.wait_ge(unit_taken, 8 * s)
                                else:
                                    pe.wait_ge(y_done, 2 * (2 * s + unit - 2))
                        if i == 0:
                            pe.wait_ge(piece_lo, 4 if first else 8 * s)
                        if i == UP:
                            pe.wait_ge(piece_lo, P0 + 4)
                        wait_lo(pe, i, s, first)
                        operands = (xTh, xTl) if i < UP else (hTh, hTl)
                        for_kinds(pe, second if i < UP else second_last, lambda nb, small: half(*operands, i % SLOTS, i % 2, bank, nb, small))
                    if first:
                        for j in (0, 1):
                            pe.wait_ge(rows_loaded[j], 32)
                        for q in (0, 1):
                            piece(P0 + q, rows, 0, q)
                        for q in (0, 1):
                            pieces2(P0 + 2 + q, rows, second_next, q)

                second = second_at(pe, 0)
                for j in (0, 1):
                    pe.wait_ge(rows_loaded[j], 16)
                for q in (0, 1):
                    piece(q, rows, 0, q, guard=False)
                for q in (0, 1):
                    pieces2(2 + q, rows, second, q)
                turn(0, True)
                with pe.Fori(1, count) as s:
                    turn(s, False)
                last = second_at(pe, count - 1)
                pe.wait_ge(hid_done, 2 * count)
                for q in (0, 1):
                    piece(8 * count + q, hid, 0, q)
                for q in (0, 1):
                    pieces2(8 * count + 2 + q, hid, last, q)
                pe.wait_ge(piece_lo, 8 * count + 4)
                for i in range(TURN - UP):
                    if i == 0:
                        pe.wait_ge(unit_taken, 8 * count)
                    if i == 2:
                        pe.wait_ge(y_done, 4 * count - 2)
                    wait_lo(pe, i, count, False)
                    for_kinds(pe, last, lambda nb, small: half(hTh, hTl, i % SLOTS, i % 2, unit_bank(i // 2), nb, small))



def combine(nc, h_rows, y_rows, final_g, gate, out):
    with ExitStack() as ctx:
        def sb(name, shape, dt=F32):
            return ctx.enter_context(nc.sbuf_tensor(name, shape, dt))

        def sem(name):
            return ctx.enter_context(nc.semaphore(name))

        BUFS, OUTS = 4, 4
        ht, yt = sb("h_again", [P, BUFS, D]), sb("y_again", [P, BUFS, TOP_K, D])
        ot, gf = sb("out_tile", [P, OUTS, D]), sb("final_rows", [P, D])
        sq = sb("out_squares", [P, D])
        ss, rms, rstd, eps = sb("out_ss", [P, TILES]), sb("out_rms", [P, TILES]), sb("out_rstd", [P, TILES]), sb("eps3", [P, 1])
        h_loaded = [sem(f"h_again_loaded{i}") for i in range(BUFS)]
        y_loaded = [[sem(f"y_again_loaded{half}{i}") for i in range(BUFS)] for half in (0, 1)]
        g_loaded, eps_set, summed, squared, rooted, inverted = (sem(n) for n in ("final_loaded", "eps3_set", "y_summed", "out_squared", "out_rooted", "out_inverted"))
        normed, stored = sem("out_normed"), [sem(f"out_stored{i}") for i in range(OUTS)]
        h_t, o_t = (a.rearrange("(t p) d -> t p d", p=P) for a in (h_rows, out))
        y_t = y_rows[0:SPARE].rearrange("(t p k) d -> t p k d", p=P, k=TOP_K)

        with nc.Block() as block:
            @block.sync
            def _(sp):
                sp.dma_start(gf[:], final_g.partition_broadcast(P)).then_inc(g_loaded, 16)
                for t in range(TILES):
                    if t >= BUFS:
                        sp.wait_ge(normed, t - BUFS + 1)
                    sp.dma_start(ht[:, t % BUFS], h_t[t]).then_inc(h_loaded[t % BUFS], 16)
                    for half in (0, 1):
                        sp.dma_start(yt[:, t % BUFS, 2 * half:2 * half + 2], y_t[t][:, 2 * half:2 * half + 2]).then_inc(y_loaded[half][t % BUFS], 16)
                for i in range(OUTS):
                    sp.wait_ge(stored[i], 16 * (TILES // OUTS))

            @block.vector
            def _(dve):
                nc.vector.memset(eps[:], EPS).then_inc(eps_set, 1)
                dve.wait_ge(g_loaded, 16)
                for t in range(TILES):
                    b = t % BUFS
                    dve.wait_ge(h_loaded[b], 16 * (t // BUFS + 1))
                    for k in range(TOP_K):
                        if k % 2 == 0:
                            dve.wait_ge(y_loaded[k // 2][b], 16 * (t // BUFS + 1))
                        if k:
                            dve.wait_ge(summed, TOP_K * t + k)
                        nc.vector.scalar_tensor_tensor(out=ht[:, b], in0=yt[:, b, k, :], scalar=gate[:, t, k:k + 1], in1=ht[:, b],
                                                       op0=ALU.mult, op1=ALU.add).then_inc(summed, 1)
                    dve.wait_ge(rooted, t + 1)
                    nc.vector.reciprocal(rstd[:, t:t + 1], rms[:, t:t + 1]).then_inc(inverted, 1)
                    dve.wait_ge(inverted, t + 1)
                    if t >= OUTS:
                        dve.wait_ge(stored[t % OUTS], 16 * (t // OUTS))
                    nc.vector.scalar_tensor_tensor(out=ot[:, t % OUTS], in0=ht[:, b], scalar=rstd[:, t:t + 1], in1=gf[:],
                                                   op0=ALU.mult, op1=ALU.mult).then_inc(normed, 1)

            @block.scalar
            def _(act):
                def store(t):
                    act.wait_ge(normed, t + 1)
                    act.dma_start(o_t[t], ot[:, t % OUTS]).then_inc(stored[t % OUTS], 16)

                act.wait_ge(eps_set, 1)
                for t in range(TILES):
                    act.wait_ge(summed, TOP_K * (t + 1))
                    nc.scalar.activation(sq[:], ht[:, t % BUFS], ACT.Square, accum_out=ss[:, t:t + 1]).then_inc(squared, 1)
                    act.wait_ge(squared, t + 1)
                    nc.scalar.activation(rms[:, t:t + 1], ss[:, t:t + 1], ACT.Sqrt, bias=eps[:], scale=1.0 / D).then_inc(rooted, 1)
                    if t:
                        store(t - 1)
                store(TILES - 1)


def make_ident(nc, ctx):
    ident = ctx.enter_context(nc.sbuf_tensor("ident", [P, P], F32))
    zeroed, done = (ctx.enter_context(nc.semaphore(n)) for n in ("ident_zeroed", "ident_done"))
    with nc.Block() as block:
        @block.gpsimd
        def _(pool):
            nc.gpsimd.memset(ident[:], 0.0).then_inc(zeroed, 1)
            pool.wait_ge(zeroed, 1)
            nc.gpsimd.affine_select(out=ident[:], in_=ident[:], compare_op=ALU.not_equal, fill=1.0, base=0,
                                    pattern=[[-1, P]], channel_multiplier=1).then_inc(done, 1)
            pool.wait_ge(done, 1)
    return ident


def build(nc, x, norm1_g, w_in, w_alpha_up, b_alpha, gla_norm_g, swa_sinks, swa_norm_g, w_out, norm2_g, w_router, b_router,
          w_glu, b_glu, w_lin, b_lin, w_down, b_down, final_g, out):
    h_rows, hn_rows, y_rows = (nc.dram_tensor(n, [r, D], F32).ap() for n, r in (("h_rows", SEQ), ("hn_rows", SEQ), ("y_rows", SPARE + GROUP_ROWS)))
    unused = nc.dram_tensor("unused_rows", [2, D], F32).ap()
    with ExitStack() as whole:
        def keep(name, shape, dt=F32):
            return whole.enter_context(nc.sbuf_tensor(name, shape, dt))

        first_sem = whole.enter_context(nc.semaphore("before_the_stages")).num + 1
        ident = make_ident(nc, whole)
        logits, gate = keep("logits", [P, TILES, EXPERTS]), keep("gate", [P, TILES, TOP_K])
        token_of, pair_of = keep("token_of", [P, BLOCKS], U32), keep("pair_of", [P, BLOCKS], U32)
        group_expert, group_second, last_group = keep("group_expert", [1, GROUPS], I32), keep("group_second", [1, GROUPS], I32), keep("last_group", [1, 1], I32)
        with ExitStack() as mixer:
            def sb(name, shape, dt=F32):
                return mixer.enter_context(nc.sbuf_tensor(name, shape, dt))

            ra = sb("ra", [P, TILES, 512])
            with ExitStack() as attention:
                def at(name, shape, stack=attention):
                    return stack.enter_context(nc.sbuf_tensor(name, shape, F32, side="right"))

                qbT, kbT, vbz = at("qbT", [P, 4, SEQ]), at("kbT", [P, 1, SEQ]), at("vbz", [P, TILES, VZ])
                with ExitStack() as gated:
                    qaT, kaT, va = (at(n, s, gated) for n, s in (("qaT", [P, PAIRS, SEQ]), ("kaT", [P, PAIRS, SEQ]), ("va", [P, TILES, 512])))
                    project(nc, x[0], norm1_g[0], w_in[0], ident, qaT, kaT, va, ra, qbT, kbT, vbz)
                    cat = sb("cat", [P, TILES, D])
                    gla(nc, w_alpha_up[0], b_alpha[0], ident, qaT, kaT, va, vbz, cat)
                wh, wl = (mixer.enter_context(nc.sbuf_tensor(n, [P, KT, D], F32R)) for n in ("w_out_hi", "w_out_lo"))
                gains, g2 = sb("head_gains", [P, D]), sb("norm2_rows", [P, D])
                w_r, b_r = sb("w_router", [P, KT, EXPERTS]), sb("b_router", [P, EXPERTS])
                swa(nc, swa_sinks[0], w_out[0], gla_norm_g[0], swa_norm_g[0], norm2_g[0], w_router[0], b_router[0], ident, qbT, kbT, vbz,
                    cat, ra, wh, wl, gains, g2, w_r, b_r)
            mix_out(nc, x[0], ident, ra, cat, wh, wl, gains, g2, w_r, b_r, logits, h_rows, hn_rows)
        w_raw = keep("w_raw", [P, RAW, 4, 512])
        w_loaded = [whole.enter_context(nc.semaphore(f"w_loaded{i}")) for i in range(RAW)]
        dispatch(nc, logits, gate, token_of, pair_of, group_expert, group_second, last_group, first_sem, (w_glu[0], w_lin[0]), w_raw, w_loaded, ident)
        experts(nc, w_raw, w_loaded, hn_rows, w_glu[0], b_glu[0], w_lin[0], b_lin[0], w_down[0], b_down[0], ident, token_of, group_expert, group_second,
                last_group, pair_of, y_rows, unused)
        combine(nc, h_rows, y_rows, final_g, gate, out[0])


_INS = ["x", "norm1_g", "w_in", "w_alpha_up", "b_alpha", "gla_norm_g", "swa_sinks", "swa_norm_g", "w_out", "norm2_g", "w_router",
        "b_router", "w_glu", "b_glu", "w_lin", "b_lin", "w_down", "b_down", "final_g"]


def kernel(**inputs):
    import numpy as np
    import concourse.bacc as bacc
    from concourse.bass_utils import run_bass_kernel_spmd

    nc = bacc.Bacc("TRN2", target_bir_lowering=False, num_devices=1)
    arrays, args = {}, []
    for name in _INS:
        a = np.ascontiguousarray(inputs[name])
        arrays[f"in_{name}"] = a
        args.append(nc.dram_tensor(f"in_{name}", a.shape, mybir.dt.from_np(a.dtype), kind="ExternalInput").ap())
    out = nc.dram_tensor("out", (1, SEQ, D), F32, kind="ExternalOutput").ap()
    build(nc, *args, out)
    r = run_bass_kernel_spmd(nc, [arrays], core_ids=[0])
    return r.results[0]["out"]
```
